# Optimizing a Trainium2 kernel written in Bass

```python
import math
import jax, jax.numpy as jnp
from jax import lax
import numpy as np

D_MODEL = 2048
BATCH = 1
SEQ = 256
DEPTH = 2

N_MIXERS = 2
N_CONV_LAYERS = (DEPTH + 1) // 2
N_GLA_LAYERS = DEPTH // 2
EPS = 1e-6
CONV_WIDTH = 31
GLA_HEADS = 4
GLA_DK = D_MODEL // 2
GLA_DV = D_MODEL
GLA_DK_HEAD = GLA_DK // GLA_HEADS
GLA_DV_HEAD = GLA_DV // GLA_HEADS
GLA_GATE_RANK = 16
GLA_GATE_NORMALIZER = 16.0
GLA_CHUNK = 64
D_FF = int(math.ceil(8 * D_MODEL / 3 / 256) * 256)

kernel_name = "hybrid_conformer_conv_gla_swiglu"

def rms_norm(x, g):
    xf = x.astype(jnp.float32)
    y = xf * lax.rsqrt(jnp.mean(xf * xf, axis=-1, keepdims=True) + EPS)
    return (y * g.astype(jnp.float32)).astype(x.dtype)

def layer_norm(x, g, b):
    xf = x.astype(jnp.float32)
    mu = jnp.mean(xf, axis=-1, keepdims=True)
    var = jnp.mean(jnp.square(xf - mu), axis=-1, keepdims=True)
    y = (xf - mu) * lax.rsqrt(var + EPS)
    return (y * g.astype(jnp.float32) + b.astype(jnp.float32)).astype(x.dtype)

def conformer_conv_module(h, w_in, b_in, w_dw, b_dw, ln_g, ln_b, w_out, b_out):
    u = h @ w_in + b_in
    a, gate = jnp.split(u, 2, axis=-1)
    u = a * jax.nn.sigmoid(gate)
    u = lax.conv_general_dilated(
        u, w_dw[:, None, :], window_strides=(1,), padding=[(CONV_WIDTH - 1, 0)],
        dimension_numbers=("NWC", "WIO", "NWC"), feature_group_count=D_MODEL) + b_dw
    u = jax.nn.silu(layer_norm(u, ln_g, ln_b))
    return u @ w_out + b_out

def _to_chunks(t):
    b, s, hh, d = t.shape
    return t.reshape(b, s // GLA_CHUNK, GLA_CHUNK, hh, d).transpose(1, 0, 3, 2, 4)

def chunked_gla(q, k, v, log_a):
    b, s, hh, dk = q.shape
    dv = v.shape[-1]
    qc, kc, vc, ac = (_to_chunks(t) for t in (q, k, v, log_a))
    causal = jnp.tril(jnp.ones((GLA_CHUNK, GLA_CHUNK), dtype=bool))[:, :, None]

    def step(state, inp):
        qi, ki, vi, ai = inp
        cum = jnp.cumsum(ai, axis=2)
        o_inter = jnp.einsum("bhcd,bhde->bhce", qi * jnp.exp(cum), state)
        diff = cum[:, :, :, None, :] - cum[:, :, None, :, :]
        decay = jnp.where(causal, jnp.exp(jnp.where(causal, diff, 0.0)), 0.0)
        scores = jnp.einsum("bhid,bhjd,bhijd->bhij", qi, ki, decay)
        o_intra = jnp.einsum("bhij,bhje->bhie", scores, vi)
        last = cum[:, :, -1:, :]
        new_state = jnp.exp(last[:, :, 0, :])[..., None] * state + jnp.einsum(
            "bhcd,bhce->bhde", ki * jnp.exp(last - cum), vi)
        return new_state, o_inter + o_intra

    state0 = jnp.zeros((b, hh, dk, dv), jnp.float32)
    _, oc = lax.scan(step, state0, (qc, kc, vc, ac))
    return oc.transpose(1, 0, 3, 2, 4).reshape(b, s, hh, dv)

def gla_mixer(h, w_in, gate_w1, gate_w2, gate_b, head_norm_g, w_out):
    b, s, _ = h.shape
    proj = h @ w_in
    q, k, v, r = jnp.split(proj, [GLA_DK, 2 * GLA_DK, 2 * GLA_DK + GLA_DV], axis=-1)
    log_a = jax.nn.log_sigmoid(((h @ gate_w1) @ gate_w2 + gate_b).astype(jnp.float32)) / GLA_GATE_NORMALIZER
    q = q.astype(jnp.float32).reshape(b, s, GLA_HEADS, GLA_DK_HEAD) * (GLA_DK_HEAD ** -0.5)
    k = k.astype(jnp.float32).reshape(b, s, GLA_HEADS, GLA_DK_HEAD)
    v = v.astype(jnp.float32).reshape(b, s, GLA_HEADS, GLA_DV_HEAD)
    log_a = log_a.reshape(b, s, GLA_HEADS, GLA_DK_HEAD)
    o = chunked_gla(q, k, v, log_a)
    o = o * lax.rsqrt(jnp.mean(o * o, axis=-1, keepdims=True) + EPS) * head_norm_g.astype(jnp.float32)
    o = o.reshape(b, s, GLA_DV).astype(h.dtype) * jax.nn.silu(r)
    return o @ w_out

def swiglu_ffn(h, w_gate_up, w_down):
    a, g = jnp.split(h @ w_gate_up, 2, axis=-1)
    return (jax.nn.silu(a) * g) @ w_down

def setup_inputs(seed: int = 0) -> dict:
    key = jax.random.key(seed)
    ks = jax.random.split(key, 24)
    f32 = jnp.float32
    D = D_MODEL

    def nrm(k, shape, scale):
        return jax.random.normal(k, shape, f32) * scale

    def gain(k, shape):
        return 1.0 + 0.02 * jax.random.normal(k, shape, f32)

    return {
        "x": jax.random.normal(ks[0], (BATCH, SEQ, D), f32),
        "norm_mix_g": gain(ks[1], (DEPTH, D)),
        "norm_ffn_g": gain(ks[2], (DEPTH, D)),
        "conv_w_in": nrm(ks[3], (N_CONV_LAYERS, D, 2 * D), D ** -0.5),
        "conv_b_in": nrm(ks[4], (N_CONV_LAYERS, 2 * D), 0.02),
        "conv_w_dw": nrm(ks[5], (N_CONV_LAYERS, CONV_WIDTH, D), CONV_WIDTH ** -0.5),
        "conv_b_dw": nrm(ks[6], (N_CONV_LAYERS, D), 0.02),
        "conv_ln_g": gain(ks[7], (N_CONV_LAYERS, D)),
        "conv_ln_b": nrm(ks[8], (N_CONV_LAYERS, D), 0.02),
        "conv_w_out": nrm(ks[9], (N_CONV_LAYERS, D, D), D ** -0.5),
        "conv_b_out": nrm(ks[10], (N_CONV_LAYERS, D), 0.02),
        "gla_w_in": nrm(ks[11], (N_GLA_LAYERS, D, 2 * GLA_DK + 2 * GLA_DV), D ** -0.5),
        "gla_gate_w1": nrm(ks[12], (N_GLA_LAYERS, D, GLA_GATE_RANK), D ** -0.5),
        "gla_gate_w2": nrm(ks[13], (N_GLA_LAYERS, GLA_GATE_RANK, GLA_DK), GLA_GATE_RANK ** -0.5),
        "gla_gate_b": nrm(ks[14], (N_GLA_LAYERS, GLA_DK), 0.1),
        "gla_head_norm_g": gain(ks[15], (N_GLA_LAYERS, GLA_HEADS, GLA_DV_HEAD)),
        "gla_w_out": nrm(ks[16], (N_GLA_LAYERS, GLA_DV, D), GLA_DV ** -0.5),
        "ffn_w_gate_up": nrm(ks[17], (DEPTH, D, 2 * D_FF), D ** -0.5),
        "ffn_w_down": nrm(ks[18], (DEPTH, D_FF, D), D_FF ** -0.5),
        "final_norm_g": gain(ks[19], (D,)),
    }

def reference(x, norm_mix_g, norm_ffn_g, conv_w_in, conv_b_in, conv_w_dw, conv_b_dw, conv_ln_g, conv_ln_b,
              conv_w_out, conv_b_out, gla_w_in, gla_gate_w1, gla_gate_w2, gla_gate_b, gla_head_norm_g,
              gla_w_out, ffn_w_gate_up, ffn_w_down, final_norm_g):
    for i in range(DEPTH):
        j = i // N_MIXERS
        h = rms_norm(x, norm_mix_g[i])
        if i % N_MIXERS == 0:
            h = conformer_conv_module(h, conv_w_in[j], conv_b_in[j], conv_w_dw[j], conv_b_dw[j],
                                      conv_ln_g[j], conv_ln_b[j], conv_w_out[j], conv_b_out[j])
        else:
            h = gla_mixer(h, gla_w_in[j], gla_gate_w1[j], gla_gate_w2[j], gla_gate_b[j],
                          gla_head_norm_g[j], gla_w_out[j])
        x = x + h
        x = x + swiglu_ffn(rms_norm(x, norm_ffn_g[i]), ffn_w_gate_up[i], ffn_w_down[i])
    return rms_norm(x, final_norm_g)


_drawn_inputs = setup_inputs


def setup_inputs(seed=0):
    import zlib

    import numpy as np

    out = dict(_drawn_inputs(seed))
    spreads = {}
    factors = {'norm_ffn_g': 2.725,
     'conv_b_in': 3.175,
     'conv_ln_g': 3.063,
     'conv_ln_b': 3.58,
     'gla_gate_b': 3.043,
     'gla_head_norm_g': 6.233,
     'final_norm_g': 2.913}
    for name, (base, spread) in spreads.items():
        noise = np.random.default_rng([zlib.crc32(name.encode()), seed]).standard_normal(out[name].shape)
        drawn = base * np.exp(spread * noise) if base else spread * noise
        out[name] = __import__('jax').numpy.asarray(drawn.astype(out[name].dtype))
    for name, factor in factors.items():
        out[name] = (out[name] * factor).astype(out[name].dtype)
    return out
```

```python
from contextlib import ExitStack

import concourse.bass as bass
from concourse import mybir

F32 = mybir.dt.float32
F32R = mybir.dt.float32r
ALU = mybir.AluOpType
ACT = mybir.ActivationFunctionType
AX_X = mybir.AxisListType.X
ds = bass.ds

P = 128
T = 256
D = 2048
KT = D // P
FF = 5632
TAPS = 31
PAD = TAPS - 1
PE_TAPS = 4
STEPS = TAPS - PE_TAPS + 2
UW = T + PE_TAPS
HEADS = 4
DK = 256
DV = 512
RANK = 16
EPS = 1e-6
GATE_DIV = 16.0
RING = 4
AHEAD = RING - 1
GW = 512
PARTS = ((0, 4), (4, 4), (8, 3))

C_CONV_IN = 0
C_CONV_OUT = C_CONV_IN + 32
C_FFN = (C_CONV_OUT + 16, C_CONV_OUT + 16 + 132 + 64)
C_QK = C_FFN[0] + 132
C_V = C_QK + 16
C_R = C_V + 16
C_GLA_OUT = C_R + 16
C_END = C_FFN[1] + 132

U_X = 0
U_CONV_IN = U_X + 4
U_CONV_OUT = U_CONV_IN + 16
U_FFN = (U_CONV_OUT + 4, U_CONV_OUT + 4 + 34 + 22)
U_QK = U_FFN[0] + 34
U_GATE = U_QK + 4
U_V = U_GATE + 2
U_PV = U_V + 4
U_R = U_PV + 4
U_GLA_OUT = U_R + 4
U_OUT = U_FFN[1] + 34

VECTORS = (("norm_mix", 32), ("norm_ffn", 32), ("conv_b_in", 32), ("conv_b_dw", 16), ("ln_g", 16),
           ("conv_b_out", 16), ("ln_b", 16), ("gate_b", 8), ("head_g", 16), ("final_g", 16))
VCOL = {}
_at = 0
for _name, _rows in VECTORS:
    VCOL[_name] = _at
    _at += _rows
VROWS = _at
LEVELS = (128, 64, 32, 16, 8, 4, 2, 1)
HID = (0, 11 + HEADS)
HID_GLA = 11
STAT = (1, 3, 4, 5, 6, 7, 8, 9, 10, 11)


def trunk(nc, x, norm_mix_g, norm_ffn_g, conv_w_in, conv_b_in, conv_w_dw, conv_b_dw, conv_ln_g, conv_ln_b,
          conv_w_out, conv_b_out, gla_w_in, gla_gate_w1, gla_gate_w2, gla_gate_b, gla_head_norm_g,
          gla_w_out, ffn_w_gate_up, ffn_w_down, final_norm_g, out):
    with ExitStack() as ctx:
        base = (nc.sbuf_base + 63) // 64 * 64

        def sb(name, shape, offset, dt=F32):
            return nc.alloc_sbuf_tensor_at(name, shape, dt, offset=base + offset)

        def sem(name):
            return ctx.enter_context(nc.semaphore(name))

        K = 1024
        res = sb("res", [P, KT, T], 0)
        x_hi = sb("x_hi", [P, KT, T], 16 * K, F32R)
        x_lo = sb("x_lo", [P, KT, T], 32 * K, F32R)
        act = sb("act", [P, KT, T], 48 * K)
        h_hi = sb("h_hi", [P, 16, T], 64 * K, F32R)
        h_lo = sb("h_lo", [P, 16, T], 80 * K, F32R)
        raw = [sb(f"raw{i}", [P, 4, GW], (96 + 8 * i) * K) for i in range(RING)]
        w_hi = [sb(f"w_hi{i}", [P, 4, GW], (128 + 8 * i) * K, F32R) for i in range(RING)]
        w_lo = [sb(f"w_lo{i}", [P, 4, GW], (160 + 8 * i) * K, F32R) for i in range(RING)]
        tmp = [sb(f"tmp{i}", [P, 4, T], (192 + 4 * i) * K) for i in range(2)]
        small = 200 * K
        vec = sb("vec", [P, VROWS], small)
        masks = sb("masks", [P, 7, 64], small + 832)
        ones = sb("ones", [P, P], small + 2624)
        ident = sb("ident", [P, P], small + 3136)
        rstd = sb("rstd", [P, T], small + 3648)
        sq_part = sb("sq_part", [P, T], small + 4672)
        sq_sum = sb("sq_sum", [P, T], small + 5696)
        eps = sb("eps", [P, 1], small + 6720)
        assert base + small + 6752 <= nc.sbuf_usable_end

        x_rows = sb("x_rows", [P, 2, D], 64 * K)
        vec_rows = sb("vec_rows", [P, 2, P], 80 * K)
        dw_rows = sb("dw_rows", [TAPS, D], 81 * K)
        dw = sb("dw", [P, KT * TAPS], 89 * K)
        u = sb("u", [P, 2, PAD + T], 64 * K)
        gate = sb("gate", [P, 2, T], 67 * K)
        y_odd = sb("y_odd", [P, T], 78 * K)
        u_hi = sb("u_hi", [P, 2, UW], 73 * K + 512, F32R)
        u_lo = sb("u_lo", [P, 2, UW], 75 * K + 768, F32R)
        diag_hi = sb("diag_hi", [P, 2, PE_TAPS, P], 80 * K, F32R)
        diag_lo = sb("diag_lo", [P, 2, PE_TAPS, P], 84 * K, F32R)
        dw_hi = sb("dw_hi", [P, KT * TAPS], 91 * K, F32R)
        dw_lo = sb("dw_lo", [P, KT * TAPS], 93 * K)
        y_sum = sb("y_sum", [P, T], 69 * K)
        ln_sq = sb("ln_sq", [P, 2, 4, T], 70 * K)
        v = sb("v", [P, 2, D], 64 * K)
        cum = sb("cum", [P, 8, T], 80 * K)
        dec = sb("dec", [P, 8, T], 88 * K)
        o_sq = sb("o_sq", [P, HEADS, 4, T], 80 * K)
        gate_w1 = sb("gate_w1", [P, KT, RANK], 192 * K)
        gate_z1 = sb("gate_z1", [RANK, T], 193 * K)
        gate_w2 = sb("gate_w2", [RANK, HEADS * DK], 194 * K)
        s_diag = sb("s_diag", [P, 2 * HEADS, P], 192 * K)
        s_off = sb("s_off", [P, HEADS, P], 196 * K)
        q_t = act[:, 0:8, :]
        k_t = act[:, 8:16, :]
        out_rows = sb("out_rows", [P, 2, D], 64 * K)

        slot = [ctx.enter_context(nc.psum_tensor(f"slot{i}", [P, 4, T], F32)) for i in range(2)]
        stat = ctx.enter_context(nc.psum_tensor("stat", [P, 2, T], F32))
        pair_s = [ctx.enter_context(nc.psum_tensor(f"pair_s{i}", [P, 512], F32)) for i in range(2)]
        misc = ctx.enter_context(nc.psum_tensor("misc", [P, 512], F32))

        raw_in = [sem(f"raw_in{i}") for i in range(RING)]
        hi_done = sem("hi_done")
        lo_done = sem("lo_done")
        w_used = sem("w_used")
        acc_read = [sem(f"acc_read{i}") for i in range(2)]
        rows_in = sem("rows_in")
        gate_in = sem("gate_in")
        consts = sem("consts")
        par_t = sem("par_t")
        par_read = sem("par_read")
        x_t = sem("x_t")
        sq_done = sem("sq_done")
        sum_done = sem("sum_done")
        stat_done = sem("stat_done")
        root_done = sem("root_done")
        rstd_done = sem("rstd_done")
        xn_done = sem("xn_done")
        xhi_done = sem("xhi_done")
        x_ready = sem("x_ready")
        sig_done = sem("sig_done")
        tap_done = sem("tap_done")
        uhi_done = sem("uhi_done")
        ulo_done = sem("ulo_done")
        diag_done = sem("diag_done")
        pe_taps = sem("pe_taps")
        dw_split = sem("dw_split")
        ysum_done = sem("ysum_done")
        part_done = sem("part_done")
        mean_done = sem("mean_done")
        cent_done = sem("cent_done")
        z_done = sem("z_done")
        hid_hi = sem("hid_hi")
        hid_ready = sem("hid_ready")
        z1_done = sem("z1_done")
        z1_read = sem("z1_read")
        z_ready = sem("z_ready")
        ls_act = sem("ls_act")
        ls_vec = sem("ls_vec")
        lev_diff = sem("lev_diff")
        lev_exp = sem("lev_exp")
        lev_mul = sem("lev_mul")
        lev_mm = sem("lev_mm")
        lev_add = sem("lev_add")
        pv_done = sem("pv_done")
        o_norm = sem("o_norm")
        out_t = sem("out_t")
        stored = sem("stored")

        block = ctx.enter_context(nc.Block())

        conv_in_w = conv_w_in[0].rearrange("(k p) n -> p k n", p=P)
        conv_out_w = conv_w_out[0].rearrange("(k p) n -> p k n", p=P)
        gla_in_w = gla_w_in[0].rearrange("(k p) n -> p k n", p=P)
        gla_out_w = gla_w_out[0].rearrange("(k p) n -> p k n", p=P)
        up_w = [ffn_w_gate_up[i].rearrange("(k p) n -> p k n", p=P) for i in range(2)]
        down_w = [ffn_w_down[i].rearrange("(k p) n -> p k n", p=P) for i in range(2)]

        def conv_view(tile):
            return tile[:, :, :].rearrange("p a (b c) -> p (a b) c", c=P)

        def over(row, n):
            return row.unsqueeze(1).broadcast_to([P, n, row.shape[1]])

        head_sq = [sq_sum[:, :], sq_part[:, :]]
        head_stat = [stat[:, 0, :], misc[:, 0:T], pair_s[0][:, 0:T], pair_s[1][:, 0:T]]

        def vcol(name, i):
            return vec[:, VCOL[name] + i:VCOL[name] + i + 1]

        @block.sync
        def _(sp):
            def rows(dst, src):
                sp.dma_start(dst, src).then_inc(rows_in, 16)

            def load(c, k, dst, src, first=False):
                if not first:
                    sp.wait_ge(lo_done, c - RING + 1)
                sp.dma_start(dst, src).then_inc(raw_in[k], 16)

            def matrix(c0, w, col0, groups, chunks=4, k0=0):
                per = 1 if chunks == RING else groups
                with sp.Fori(0, groups // per) as g:
                    for j in range(per * chunks):
                        load(c0 + per * chunks * g + j, j % RING, raw[j % RING][:, :, :],
                             w[:, k0 + 4 * (j % chunks):k0 + 4 * (j % chunks) + 4,
                               ds(col0 + GW * (g * per + j // chunks), GW)])

            rows(x_rows[:, :, :], x[0].rearrange("(a p) d -> p a d", p=P))
            at = 0
            for name, src in (("norm_mix", norm_mix_g), ("norm_ffn", norm_ffn_g), ("conv_b_in", conv_b_in),
                              ("conv_b_dw", conv_b_dw), ("ln_g", conv_ln_g)):
                n = dict(VECTORS)[name]
                rows(vec_rows[at:at + n, 0, :], src.rearrange("a (r c) -> (a r) c", c=P))
                at += n
            assert at == P
            at = 0
            for name, src in (("conv_b_out", conv_b_out), ("ln_b", conv_ln_b), ("gate_b", gla_gate_b),
                              ("head_g", gla_head_norm_g[0]), ("final_g", final_norm_g.rearrange("(a d) -> a d", a=1))):
                n = dict(VECTORS)[name]
                rows(vec_rows[at:at + n, 1, :], src.rearrange("a (r c) -> (a r) c", c=P))
                at += n
            rows(dw_rows[:, :], conv_w_dw[0])

            def conv_turn(i, i0, first):
                for t in range(2):
                    for h in range(2):
                        k = 2 * t + h
                        src = conv_in_w[:, :, ds(2 * P * i + (2 * P * i0 + P * t + D * (1 - h)), P)]
                        load(4 * i + (4 * i0 + k), k, conv_view(raw[k]), src, first)

            conv_turn(0, 0, True)
            with sp.Fori(0, KT // 2 - 1) as i:
                conv_turn(i, 1, False)
            matrix(C_CONV_OUT, conv_out_w, 0, 4)

            def ffn(l):
                for pt, (first, pairs) in enumerate(PARTS):
                    c0 = C_FFN[l] + 48 * pt
                    with sp.Fori(0, pairs) as p:
                        for half in range(2):
                            for j in range(4):
                                load(c0 + 8 * p + 4 * half + j, j, raw[j][:, :, :],
                                     up_w[l][:, 4 * j:4 * j + 4, ds(half * FF + GW * first + GW * p, GW)])
                    matrix(c0 + 8 * pairs, down_w[l], 0, 4, chunks=pairs, k0=4 * first)

            ffn(0)
            matrix(C_QK, gla_in_w, 0, 12)
            matrix(C_GLA_OUT, gla_out_w, 0, 4)
            ffn(1)

            for a in range(2):
                sp.wait_ge(acc_read[0], U_OUT // 2 + a + 1)
                sp.wait_ge(acc_read[1], U_OUT // 2 + a + 1)
                sp.dma_start(out[0, a * P:(a + 1) * P, :], out_rows[:, a, :]).then_inc(stored, 16)
            sp.wait_ge(stored, 32)

        @block.gpsimd
        def _(pool):
            def lo(c, k, wait_order=False):
                if wait_order:
                    pool.wait_ge(lo_done, c)
                pool.wait_ge(hi_done, c + 1)
                nc.gpsimd.tensor_tensor(w_lo[k][:, :, :], raw[k][:, :, :], w_hi[k][:, :, :].bitcast(F32),
                                        ALU.subtract).then_inc(lo_done, 1)

            nc.gpsimd.memset(ident[:, :], 0.0).then_inc(consts, 1)
            nc.gpsimd.memset(ones[:, :], 1.0).then_inc(consts, 1)
            nc.gpsimd.memset(eps[:, :], EPS).then_inc(consts, 1)
            nc.gpsimd.memset(masks[:, :, :], 1.0).then_inc(consts, 1)
            pool.wait_ge(consts, 4)
            nc.gpsimd.affine_select(out=ident[:, :], in_=ident[:, :], compare_op=ALU.not_equal, fill=1.0,
                                    base=0, pattern=[[-1, P]], channel_multiplier=1).then_inc(consts, 1)
            n = 5
            for m, s in enumerate(LEVELS[1:]):
                v3 = masks[:, m, :].rearrange("p (b r) -> p b r", r=s)
                nc.gpsimd.affine_select(out=v3, in_=v3, compare_op=ALU.is_ge, fill=0.0, base=0,
                                        pattern=[[-2 * s, 64 // s], [0, s]], channel_multiplier=1).then_inc(consts, 1)
                n += 1
                pool.wait_ge(consts, n)
                nc.gpsimd.affine_select(out=v3, in_=v3, compare_op=ALU.is_ge, fill=0.0, base=s - 1,
                                        pattern=[[2 * s, 64 // s], [0, s]], channel_multiplier=-1).then_inc(consts, 1)
                n += 1
            for c in range(AHEAD):
                lo(c, c)
            def lo_turn(i):
                for j in range(AHEAD, AHEAD + 4):
                    lo(4 * i + j, j % RING)

            def sum_y(tile, done):
                pool.wait_ge(tap_done, done)
                pool.wait_ge(ysum_done, tile + 1)
                nc.gpsimd.tensor_tensor(y_sum[:, :], y_sum[:, :], act[:, ds(tile, 1), :].rearrange("p a t -> p (a t)"),
                                        ALU.add).then_inc(ysum_done, 1)

            lo_turn(0)
            with pool.Fori(0, KT // 2 - 1) as i:
                for t in range(2):
                    for h in range(2):
                        j = 2 * t + h + AHEAD
                        lo(4 * i + (4 + j), j % RING)
                    sum_y(2 * i + t, 2 * STEPS * i + (STEPS * (t + 1) + 2))
            for t in range(KT - 2, KT):
                sum_y(t, STEPS * (t + 1) + 2)
            pool.wait_ge(sum_done, 16)
            pool.dma_start(gate_w1[:, :, :], gla_gate_w1[0].rearrange("(k p) r -> p k r", p=P)).then_inc(gate_in, 16)
            pool.dma_start(gate_w2[:, :], gla_gate_w2[0]).then_inc(gate_in, 16)
            for j in range(16):
                lo(C_V + AHEAD + j, (AHEAD + j) % RING, wait_order=(j == 0))

        @block.scalar
        def _(scalar):
            def hi(c4, k):
                scalar.wait_ge(raw_in[k], 16 * c4 + 16)
                if not (isinstance(c4, int) and c4 == 0):
                    scalar.wait_ge(w_used, 4 * c4 + k - RING + 1)
                nc.scalar.activation(w_hi[k][:, :, :], raw[k][:, :, :], ACT.Copy).then_inc(hi_done, 1)

            def hi_group(c0, chunks=4):
                for c in range(c0 + AHEAD, min(c0 + AHEAD + chunks, C_END)):
                    hi(c // RING, c % RING)

            def hi_group_at(c4):
                for j in range(AHEAD, AHEAD + 4):
                    hi(c4 + j // RING, j % RING)

            def root(n, use, scale):
                scalar.wait_ge(stat_done, STAT[n])
                nc.scalar.activation(rstd[:, :], stat[:, use, :], ACT.Sqrt, bias=eps[:, 0:1],
                                     scale=scale).then_inc(root_done, 1)

            def split_tiles(n):
                for t in range(KT):
                    scalar.wait_ge(xn_done, n + t + 1)
                    nc.scalar.activation(x_hi[:, t, :], act[:, t, :], ACT.Copy).then_inc(xhi_done, 1)

            def squares(use0, n0, g):
                scalar.wait_ge(acc_read[g % 2], (use0 + g) // 2 + 1)
                if g >= 2:
                    scalar.wait_ge(sum_done, n0 + g - 1)
                nc.scalar.activation(tmp[g % 2][:, :, :], res[:, 4 * g:4 * g + 4, :], ACT.Square).then_inc(sq_done, 1)

            for g in range(4):
                squares(U_X, 0, g)
            for c in range(AHEAD):
                hi(0, c)
            root(0, 0, 1.0 / D)
            split_tiles(0)

            def diagonals(tile, t):
                for j in range(PE_TAPS):
                    for parts, weights in ((diag_hi, dw), (diag_lo, dw_lo)):
                        ins = nc.scalar.activation(parts[:, t, j, :], ident[:, :], ACT.Copy,
                                                   scale=weights[:, ds(TAPS * tile + j, 1)])
                ins.then_inc(diag_done, 1)

            def conv_turn(i):
                for t in range(2):
                    j = 2 * t + AHEAD
                    hi(i + j // RING, j % RING)
                    scalar.wait_ge(w_used, 4 * i + 2 * t + 1)
                    scalar.wait_ge(acc_read[t], U_CONV_IN // 2 + i)
                    nc.scalar.activation(gate[:, t, :], slot[t][:, 2, :], ACT.Sigmoid,
                                         bias=vec[:, ds(VCOL["conv_b_in"] + KT + t + 2 * i, 1)]).then_inc(sig_done, 1)
                    if not (isinstance(i, int) and i == 0):
                        scalar.wait_ge(pe_taps, 2 * i + t - 1)
                    diagonals(2 * i + t, t)
                    hi(i + (j + 1) // RING, (j + 1) % RING)
                    scalar.wait_ge(acc_read[t], U_CONV_IN // 2 + 1 + i)
                    nc.scalar.activation(u_hi[:, t, :], u[:, t, 0:UW], ACT.Copy).then_inc(uhi_done, 1)

            scalar.wait_ge(par_read, 2)
            nc.scalar.activation(dw_hi[:, :], dw[:, :], ACT.Copy).then_inc(dw_split, 1)
            scalar.wait_ge(dw_split, 2)
            conv_turn(0)
            with scalar.Fori(1, KT // 2) as i:
                conv_turn(i)
            for g in range(4):
                scalar.wait_ge(cent_done, g + 1)
                if g >= 2:
                    scalar.wait_ge(sum_done, 4 + g - 1)
                nc.scalar.activation(ln_sq[:, g % 2, :, :], act[:, 4 * g:4 * g + 4, :], ACT.Square).then_inc(sq_done, 1)
            root(1, 1, 1.0 / D)
            for t in range(KT):
                if t % 4 == 0:
                    scalar.wait_ge(z_done, t // 4 + 1)
                nc.scalar.activation(act[:, t, :], act[:, t, :], ACT.Silu, bias=vcol("ln_b", t),
                                     scale=vcol("ln_g", t)).then_inc(xn_done, 1)
                scalar.wait_ge(xn_done, KT + t + 1)
                nc.scalar.activation(x_hi[:, t, :], act[:, t, :], ACT.Copy).then_inc(xhi_done, 1)
            for g in range(4):
                hi_group(C_CONV_OUT + 4 * g)
                squares(U_CONV_OUT, 8, g)
            root(2, 0, 1.0 / D)
            split_tiles(2 * KT)

            def ffn(l, n_sq, n_root, n_split, last):
                for pt, (first, pairs) in enumerate(PARTS):
                    c0, u0 = C_FFN[l] + 48 * pt, U_FFN[l] + 12 * pt
                    with scalar.Fori(0, pairs) as p:
                        hi_group_at(c0 // 4 + 2 * p)
                        scalar.wait_ge(w_used, c0 + 8 * p + 4)
                        scalar.wait_ge(acc_read[1], u0 // 2 + p)
                        nc.scalar.activation(tmp[0][:, :, :], slot[0][:, :, :], ACT.Silu).then_inc(acc_read[0], 1)
                        hi_group_at(c0 // 4 + 1 + 2 * p)
                        scalar.wait_ge(acc_read[1], u0 // 2 + p + 1)
                        nc.scalar.activation(h_hi[:, ds(4 * p, 4), :], tmp[1][:, :, :], ACT.Copy).then_inc(hid_hi, 1)
                    d0, du = c0 + 8 * pairs, u0 + 2 * pairs
                    if pt < 2:
                        with scalar.Fori(0, 4) as g:
                            hi_group_at(d0 // 4 + g)
                    else:
                        for g in range(4):
                            hi_group(d0 + pairs * g, pairs)
                            squares(du, n_sq, g)
                root(n_root, 0, 1.0 / D)
                if not last:
                    split_tiles(n_split)

            ffn(0, 12, 3, 3 * KT, False)

            scalar.wait_ge(z1_done, 1)
            nc.scalar.activation(gate_z1[:, :], misc[0:RANK, 0:T], ACT.Copy).then_inc(z1_read, 1)
            for g in range(4):
                hi_group(C_QK + 4 * g)
                scalar.wait_ge(w_used, C_QK + 4 * g + 4)
                nc.scalar.activation(act[:, 4 * g:4 * g + 4, :], slot[g % 2][:, :, :], ACT.Copy,
                                     scale=DK ** -0.5 if g < 2 else 1.0).then_inc(acc_read[g % 2], 1)
            scalar.wait_ge(acc_read[0], U_GATE // 2 + 1)
            scalar.wait_ge(acc_read[1], U_GATE // 2 + 1)
            nc.scalar.activation(dec[:, :, :], cum[:, :, :], ACT.Abs).then_inc(ls_act, 1)
            scalar.wait_ge(ls_act, 1)
            nc.scalar.activation(dec[:, :, :], dec[:, :, :], ACT.Exp, scale=-1.0).then_inc(ls_act, 1)
            scalar.wait_ge(ls_act, 2)
            nc.scalar.activation(dec[:, :, :], dec[:, :, :], ACT.Ln, bias=1.0).then_inc(ls_act, 1)

            def level_exp(n):
                scalar.wait_ge(lev_diff, 2 * (n + 1))
                nc.scalar.activation(dec[:, :, :], dec[:, :, :], ACT.Exp, scale=1.0 / GATE_DIV).then_inc(lev_exp, 1)

            for g in range(4):
                for j in range(4):
                    c = C_V + 4 * g + j + AHEAD
                    hi(c // RING, c % RING)
                    if j % 2 == 0:
                        level_exp(2 * g + j // 2)
                scalar.wait_ge(w_used, C_V + 4 * g + 4)
                nc.scalar.activation(v[:, :, g * DV:(g + 1) * DV],
                                     slot[g % 2][:, :, :].rearrange("p (a b) t -> p a (b t)", a=2),
                                     ACT.Copy).then_inc(acc_read[g % 2], 1)
            scalar.wait_ge(lev_mm, len(LEVELS) + 1)
            for h in range(HEADS):
                scalar.wait_ge(acc_read[h % 2], (U_PV + h) // 2 + 1)
                nc.scalar.activation(o_sq[:, h, :, :], act[:, 4 * h:4 * h + 4, :], ACT.Square).then_inc(sq_done, 1)
            for h in range(HEADS):
                if h >= 1:
                    scalar.wait_ge(o_norm, h)
                scalar.wait_ge(stat_done, STAT[4 + h])
                nc.scalar.activation(rstd[:, :], head_stat[h], ACT.Sqrt, bias=eps[:, 0:1],
                                     scale=1.0 / DV).then_inc(root_done, 1)
            for h in range(HEADS):
                hi_group(C_R + 4 * h)
                scalar.wait_ge(w_used, C_R + 4 * h + 4)
                if h == 0:
                    scalar.wait_ge(pv_done, HEADS)
                else:
                    scalar.wait_ge(z_done, 4 + h)
                nc.scalar.activation(tmp[0][:, :, :], slot[h % 2][:, :, :], ACT.Silu).then_inc(acc_read[h % 2], 1)
                scalar.wait_ge(z_done, 4 + h + 1)
                nc.scalar.activation(h_hi[:, 4 * h:4 * h + 4, :], tmp[1][:, :, :], ACT.Copy).then_inc(hid_hi, 1)
            for g in range(4):
                hi_group(C_GLA_OUT + 4 * g)
                squares(U_GLA_OUT, 20, g)
            root(8, 0, 1.0 / D)
            split_tiles(4 * KT)
            ffn(1, 24, 9, 5 * KT, True)
            for n in range(2):
                scalar.wait_ge(out_t, 2 * n + 2)
                nc.scalar.activation(out_rows[:, n, 1024:2048].rearrange("p (b t) -> p b t", t=T), slot[1][:, :, :],
                                     ACT.Copy).then_inc(acc_read[1], 1)

        @block.vector
        def _(dve):
            def lo(c, k, wait_order=False):
                if wait_order:
                    dve.wait_ge(lo_done, c)
                dve.wait_ge(hi_done, c + 1)
                nc.vector.tensor_tensor(w_lo[k][:, :, :], raw[k][:, :, :], w_hi[k][:, :, :].bitcast(F32),
                                        ALU.subtract).then_inc(lo_done, 1)

            def lo_group(c0, chunks=4, wait_order=False):
                for j in range(chunks):
                    c = c0 + AHEAD + j
                    if c < C_END:
                        lo(c, c % RING, wait_order and j == 0)

            def lo_group_at(c0, g, step):
                for j in range(4):
                    lo(c0 + AHEAD + j + step * g, (AHEAD + j) % RING)

            def sum_squares(n0, g, src):
                dve.wait_ge(sq_done, n0 + g + 1)
                if g == 0:
                    nc.vector.tensor_reduce(sq_sum[:, :], src.rearrange("p k t -> p t k"), AX_X, ALU.add).then_inc(sum_done, 1)
                    return
                dve.wait_ge(sum_done, n0 + g)
                nc.vector.tensor_reduce(sq_part[:, :], src.rearrange("p k t -> p t k"), AX_X, ALU.add).then_inc(part_done, 1)
                parts[0] += 1
                dve.wait_ge(part_done, parts[0])
                nc.vector.tensor_tensor(sq_sum[:, :], sq_sum[:, :], sq_part[:, :], ALU.add).then_inc(sum_done, 1)

            def invert(n):
                dve.wait_ge(root_done, n + 1)
                nc.vector.reciprocal(rstd[:, :], rstd[:, :]).then_inc(rstd_done, 1)
                dve.wait_ge(rstd_done, n + 1)

            def rms_tiles(name, v0, n):
                def remainder(t):
                    dve.wait_ge(xhi_done, n + t + 1)
                    nc.vector.tensor_tensor(x_lo[:, t, :], act[:, t, :], x_hi[:, t, :].bitcast(F32),
                                            ALU.subtract).then_inc(x_ready, 1)

                for t in range(KT):
                    nc.vector.scalar_tensor_tensor(out=act[:, t, :], in0=res[:, t, :], scalar=vcol(name, v0 + t),
                                                   in1=rstd[:, :], op0=ALU.mult, op1=ALU.mult).then_inc(xn_done, 1)
                    if t >= 1:
                        remainder(t - 1)
                remainder(KT - 1)

            parts = [0]

            dve.wait_ge(par_t, 1)
            nc.vector.tensor_copy(vec[:, :], misc[:, 0:VROWS]).then_inc(par_read, 1)
            dve.wait_ge(par_t, 2)
            nc.vector.tensor_copy(dw[:, :], pair_s[0][:, 0:KT * TAPS]).then_inc(par_read, 1)
            for g in range(4):
                dve.wait_ge(x_t, g + 1)
                nc.vector.tensor_copy(res[:, 4 * g:4 * g + 4, :], slot[g % 2][:, :, :]).then_inc(acc_read[g % 2], 1)
                if g >= 1:
                    sum_squares(0, g - 1, tmp[(g - 1) % 2][:, :, :])
            sum_squares(0, 3, tmp[1][:, :, :])
            invert(0)
            rms_tiles("norm_mix", 0, 0)

            dve.wait_ge(x_t, 4)
            nc.vector.memset(y_sum[:, :], 0.0).then_inc(ysum_done, 1)
            nc.vector.memset(u[:, 0, 0:PAD], 0.0).then_inc(tap_done, 1)
            nc.vector.memset(u[:, 1, 0:PAD], 0.0).then_inc(tap_done, 1)
            def conv_tile(i, t):
                y = act[:, ds(2 * i + t, 1), :].rearrange("p a t -> p (a t)")
                done = STEPS * t + 2 + 2 * STEPS * i
                dve.wait_ge(sig_done, 2 * i + t + 1)
                dve.wait_ge(w_used, 4 * i + 2 * t + 2)
                dve.wait_ge(tap_done, done)
                if not (isinstance(i, int) and i == 0):
                    dve.wait_ge(uhi_done, 2 * i + t - 1)
                nc.vector.scalar_tensor_tensor(out=u[:, t, PAD:PAD + T], in0=slot[t][:, 0, :],
                                               scalar=vec[:, ds(VCOL["conv_b_in"] + t + 2 * i, 1)],
                                               in1=gate[:, t, :], op0=ALU.add, op1=ALU.mult).then_inc(acc_read[t], 1)
                dve.wait_ge(acc_read[t], U_CONV_IN // 2 + i + 1)
                for n, j in enumerate(range(PE_TAPS, TAPS)):
                    acc = (y, y_odd[:, :])[n % 2]
                    w = dw[:, ds(TAPS * (2 * i + t) + j, 1)]
                    if n == 0:
                        nc.vector.tensor_scalar(acc, u[:, t, j:j + T], w, vec[:, ds(VCOL["conv_b_dw"] + t + 2 * i, 1)],
                                                ALU.mult, ALU.add).then_inc(tap_done, 1)
                    elif n == 1:
                        nc.vector.tensor_scalar(acc, u[:, t, j:j + T], w, None, ALU.mult).then_inc(tap_done, 1)
                    else:
                        dve.wait_ge(tap_done, done + n - 1)
                        nc.vector.scalar_tensor_tensor(out=acc, in0=u[:, t, j:j + T], scalar=w, in1=acc,
                                                       op0=ALU.mult, op1=ALU.add).then_inc(tap_done, 1)
                    if n == 2:
                        dve.wait_ge(uhi_done, 2 * i + t + 1)
                        nc.vector.tensor_tensor(u_lo[:, t, :], u[:, t, 0:UW], u_hi[:, t, :].bitcast(F32),
                                                ALU.subtract).then_inc(ulo_done, 1)
                dve.wait_ge(pe_taps, 2 * i + t + 1)
                early = (y, y_odd[:, :])[(STEPS - 3 + 1) % 2]
                dve.wait_ge(tap_done, done + STEPS - 3)
                nc.vector.tensor_tensor(early, pair_s[t][:, 0:T], early, ALU.add).then_inc(tap_done, 1)
                dve.wait_ge(tap_done, done + STEPS - 1)
                nc.vector.tensor_tensor(y, y, y_odd[:, :], ALU.add).then_inc(tap_done, 1)

            dve.wait_ge(dw_split, 1)
            nc.vector.tensor_tensor(dw_lo[:, :], dw[:, :], dw_hi[:, :].bitcast(F32), ALU.subtract).then_inc(dw_split, 1)
            for t in range(2):
                conv_tile(0, t)
            with dve.Fori(1, KT // 2) as i:
                for t in range(2):
                    conv_tile(i, t)

            dve.wait_ge(stat_done, STAT[1] - 1)
            nc.vector.tensor_scalar(rstd[:, :], stat[:, 0, :], 1.0 / D, None, ALU.mult).then_inc(mean_done, 1)
            dve.wait_ge(mean_done, 1)
            for g in range(4):
                nc.vector.tensor_tensor(act[:, 4 * g:4 * g + 4, :], act[:, 4 * g:4 * g + 4, :], over(rstd[:, :], 4),
                                        ALU.subtract).then_inc(cent_done, 1)
                if g >= 1:
                    sum_squares(4, g - 1, ln_sq[:, (g - 1) % 2, :, :])
            sum_squares(4, 3, ln_sq[:, 1, :, :])
            invert(1)

            def ln_remainder(t):
                dve.wait_ge(xhi_done, KT + t + 1)
                nc.vector.tensor_tensor(x_lo[:, t, :], act[:, t, :], x_hi[:, t, :].bitcast(F32),
                                        ALU.subtract).then_inc(x_ready, 1)
            for g in range(4):
                nc.vector.tensor_tensor(act[:, 4 * g:4 * g + 4, :], act[:, 4 * g:4 * g + 4, :], over(rstd[:, :], 4),
                                        ALU.mult).then_inc(z_done, 1)
                if g >= 1:
                    for t in range(4 * g - 4, 4 * g):
                        ln_remainder(t)
            for t in range(12, 16):
                ln_remainder(t)

            def residual_group(c_end, use, g, bias=None):
                dve.wait_ge(w_used, c_end + 1)
                if bias is None:
                    nc.vector.tensor_tensor(res[:, ds(4 * g, 4), :], slot[use % 2][:, :, :], res[:, ds(4 * g, 4), :],
                                            ALU.add).then_inc(acc_read[use % 2], 1)
                    return
                for b in range(4):
                    ins = nc.vector.scalar_tensor_tensor(out=res[:, 4 * g + b, :], in0=slot[use % 2][:, b, :],
                                                         scalar=vcol(bias, 4 * g + b), in1=res[:, 4 * g + b, :],
                                                         op0=ALU.add, op1=ALU.add)
                ins.then_inc(acc_read[use % 2], 1)

            def residual_and_squares(c0, use0, n0, chunks=4, bias=None, order=False):
                for g in range(4):
                    lo_group(c0 + chunks * g, chunks, wait_order=order and g == 0)
                    residual_group(c0 + chunks * (g + 1) - 1, use0 + g, g, bias)
                    if g >= 1:
                        sum_squares(n0, g - 1, tmp[(g - 1) % 2][:, :, :])
                sum_squares(n0, 3, tmp[1][:, :, :])

            residual_and_squares(C_CONV_OUT, U_CONV_OUT, 8, bias="conv_b_out", order=True)
            invert(2)
            rms_tiles("norm_ffn", 0, 2 * KT)

            def ffn(l, n_sq):
                for pt, (first, pairs) in enumerate(PARTS):
                    c0, u0, h0 = C_FFN[l] + 48 * pt, U_FFN[l] + 12 * pt, HID[l] + first
                    with dve.Fori(0, pairs) as p:
                        lo_group_at(c0, p, 8)
                        lo_group_at(c0 + 4, p, 8)
                        dve.wait_ge(w_used, c0 + 8 * p + 8)
                        dve.wait_ge(acc_read[0], u0 // 2 + p + 1)
                        nc.vector.tensor_tensor(tmp[1][:, :, :], slot[1][:, :, :], tmp[0][:, :, :],
                                                ALU.mult).then_inc(acc_read[1], 1)
                        dve.wait_ge(hid_hi, h0 + p + 1)
                        nc.vector.tensor_tensor(h_lo[:, ds(4 * p, 4), :], tmp[1][:, :, :],
                                                h_hi[:, ds(4 * p, 4), :].bitcast(F32), ALU.subtract).then_inc(hid_ready, 1)
                    d0, du = c0 + 8 * pairs, u0 + 2 * pairs
                    if pt < 2:
                        with dve.Fori(0, 2) as i:
                            for g in range(2):
                                lo_group_at(d0 + 4 * g, i, 8)
                                residual_group(d0 + 4 * g + 3 + 8 * i, g, 2 * i + g)
                    else:
                        residual_and_squares(d0, du, n_sq, chunks=pairs)

            ffn(0, 12)
            invert(3)
            rms_tiles("norm_mix", KT, 3 * KT)

            for g in range(4):
                lo_group(C_QK + 4 * g)
            for n in range(2):
                dve.wait_ge(z_ready, n + 1)
                for b in range(4):
                    ins = nc.vector.tensor_scalar(cum[:, 4 * n + b, :], slot[n][:, b, :], vcol("gate_b", 4 * n + b), None,
                                                  ALU.add)
                ins.then_inc(acc_read[n], 1)
            nc.vector.memset(sq_part[:, :], 1.0).then_inc(ls_vec, 1)
            dve.wait_ge(ls_act, 3)
            nc.vector.scalar_tensor_tensor(out=cum[:, :, :], in0=cum[:, :, :], scalar=0.0, in1=dec[:, :, :],
                                           op0=ALU.min, op1=ALU.subtract).then_inc(ls_vec, 1)
            dve.wait_ge(ls_vec, 2)
            for t in range(8):
                ins = nc.vector.tensor_tensor_scan(out=cum[:, t, :], data0=sq_part[:, :], data1=cum[:, t, :],
                                                   initial=0.0, op0=ALU.mult, op1=ALU.add)
            ins.then_inc(ls_vec, 1)
            dve.wait_ge(ls_vec, 3)

            adds = [0]

            def step(ins):
                ins.then_inc(lev_add, 1)
                adds[0] += 1

            def halves(tile, s):
                return tile.rearrange("p k (b h r) -> p (k b) h r", h=2, r=s)

            def level_exponents(n):
                s = LEVELS[n]
                c, d = halves(cum[:, :, :], s), halves(dec[:, :, :], s)
                blocks = 8 * T // (2 * s)
                ref = c[:, :, 0, s - 1:s].broadcast_to([P, blocks, s])
                if n >= 1:
                    dve.wait_ge(lev_mm, n + 1)
                nc.vector.tensor_tensor(d[:, :, 0, :], ref, c[:, :, 0, :], ALU.subtract).then_inc(lev_diff, 1)
                nc.vector.tensor_tensor(d[:, :, 1, :], c[:, :, 1, :], ref, ALU.subtract).then_inc(lev_diff, 1)

            def level_operands(n):
                s = LEVELS[n]
                d, q, k = (halves(z, s) for z in (dec[:, :, :], q_t, k_t))
                dve.wait_ge(lev_exp, n + 1)
                nc.vector.tensor_tensor(d[:, :, 0, :], d[:, :, 0, :], k[:, :, 0, :], ALU.mult).then_inc(lev_mul, 1)
                nc.vector.tensor_tensor(d[:, :, 1, :], d[:, :, 1, :], q[:, :, 1, :], ALU.mult).then_inc(lev_mul, 1)

            def level_add(n):
                s = LEVELS[n]
                dve.wait_ge(lev_mm, n + 2)
                if n == 0:
                    step(nc.vector.tensor_copy(s_off[:, :, :], pair_s[1][:, :].rearrange("p (h i) -> p h i", i=P)))
                    return
                pr = pair_s[(n + 1) % 2][:, :].rearrange("p (h i) -> p h i", i=64)
                mask = masks[:, n - 1:n, :].broadcast_to([P, 8, 64])
                step(nc.vector.tensor_tensor(pr, pr, mask, ALU.mult))
                dve.wait_ge(lev_add, adds[0])
                sd = s_diag[:, :, :].rearrange("p k (b h r) -> p (k b) h r", h=2, r=s)[:, :, 1, :]
                pr2 = pair_s[(n + 1) % 2][:, :].rearrange("p (b r) -> p b r", r=s)
                step(nc.vector.tensor_tensor(sd, sd, pr2, ALU.add))

            dve.wait_ge(lev_mm, 1)
            dve.wait_ge(consts, 19)
            for a in range(2):
                step(nc.vector.tensor_tensor(s_diag[:, 4 * a:4 * a + 4, :], pair_s[a][:, :].rearrange("p (h i) -> p h i", i=P),
                                             over(ident[:, :], 4),
                                             ALU.mult))
            dve.wait_ge(lev_add, 2)
            for n in range(len(LEVELS)):
                level_exponents(n)
                if n >= 1:
                    level_add(n - 1)
                level_operands(n)
            level_add(len(LEVELS) - 1)

            def head_sum(h):
                dve.wait_ge(sq_done, 16 + h + 1)
                if h >= 2:
                    dve.wait_ge(stat_done, STAT[4 + h - 2])
                nc.vector.tensor_reduce(head_sq[h % 2], o_sq[:, h, :, :].rearrange("p k t -> p t k"), AX_X,
                                        ALU.add).then_inc(sum_done, 1)

            for h in range(HEADS):
                dve.wait_ge(pv_done, h + 1)
                nc.vector.tensor_copy(act[:, 4 * h:4 * h + 4, :], slot[h % 2][:, :, :]).then_inc(acc_read[h % 2], 1)
                if h >= 1:
                    head_sum(h - 1)
            head_sum(HEADS - 1)
            for h in range(HEADS):
                invert(4 + h)
                for b in range(4):
                    ins = nc.vector.scalar_tensor_tensor(out=act[:, 4 * h + b, :], in0=act[:, 4 * h + b, :],
                                                         scalar=vcol("head_g", 4 * h + b), in1=rstd[:, :],
                                                         op0=ALU.mult, op1=ALU.mult)
                ins.then_inc(o_norm, 1)
            for h in range(HEADS):
                lo_group(C_R + 4 * h, wait_order=(h == 0))
                dve.wait_ge(acc_read[h % 2], (U_R + h) // 2 + 1)
                dve.wait_ge(o_norm, h + 1)
                nc.vector.tensor_tensor(tmp[1][:, :, :], tmp[0][:, :, :], act[:, 4 * h:4 * h + 4, :],
                                        ALU.mult).then_inc(z_done, 1)
                dve.wait_ge(hid_hi, HID_GLA + h + 1)
                nc.vector.tensor_tensor(h_lo[:, 4 * h:4 * h + 4, :], tmp[1][:, :, :],
                                        h_hi[:, 4 * h:4 * h + 4, :].bitcast(F32), ALU.subtract).then_inc(hid_ready, 1)
            residual_and_squares(C_GLA_OUT, U_GLA_OUT, 20)
            invert(8)
            rms_tiles("norm_ffn", KT, 4 * KT)
            ffn(1, 24)
            invert(9)
            for t in range(KT):
                nc.vector.scalar_tensor_tensor(out=act[:, t, :], in0=res[:, t, :], scalar=vcol("final_g", t),
                                               in1=rstd[:, :], op0=ALU.mult, op1=ALU.mult).then_inc(xn_done, 1)
            for n in range(2):
                dve.wait_ge(out_t, 2 * n + 1)
                nc.vector.tensor_copy(out_rows[:, n, 0:1024].rearrange("p (b t) -> p b t", t=T),
                                      slot[0][:, :, :]).then_inc(acc_read[0], 1)

        @block.tensor
        def _(pe):
            mm = nc.tensor.matmul

            def free_slot(s, use2):
                pe.wait_ge(acc_read[s], use2)

            def chunk(k, s, x1, x2, k0, first, last, ready=None):
                for kt in range(4):
                    if ready is not None:
                        pe.wait_ge(ready[0], ready[1] + kt * ready[2] + 1)
                    for nb in range(4):
                        cols = slice(nb * P, nb * P + P)
                        for i, (w, xx) in enumerate(((w_hi, x1), (w_hi, x2), (w_lo, x1))):
                            ins = mm(slot[s][:, nb, :], w[k][:, kt, cols], xx[:, k0 + kt, :],
                                     start=(first and kt == 0 and i == 0 and nb % 2 == 0),
                                     stop=(last and kt == 3 and i == 2), skip_group_check=True)
                ins.then_inc(w_used, 1)

            def group(c0, k0, s, chunks, x1, x2, ready, per_chunk=False):
                for j in range(chunks):
                    pe.wait_ge(lo_done, c0 + j + 1)
                    if per_chunk:
                        pe.wait_ge(ready[0], ready[1] + j + 1)
                        rd = None
                    else:
                        rd = (ready[0], ready[1] + 4 * j, 1)
                    chunk((k0 + j) % RING, s, x1, x2, 4 * j, j == 0, j == chunks - 1, rd)

            def statistic(to, src, ready, count):
                pe.wait_ge(ready, count)
                mm(to, ones[:, :], src, start=True, stop=True).then_inc(stat_done, 1)

            pe.wait_ge(consts, 5)
            pe.wait_ge(rows_in, 16 * 12)
            nc.tensor.transpose(misc[:, 0:P], vec_rows[:, 0, :], ident[:, :])
            nc.tensor.transpose(misc[:, P:VROWS], vec_rows[0:VROWS - P, 1, :], ident[0:VROWS - P, 0:VROWS - P]).then_inc(par_t, 1)
            for k in range(KT):
                ins = nc.tensor.transpose(pair_s[0][:, k * TAPS:(k + 1) * TAPS], dw_rows[:, k * P:(k + 1) * P],
                                          ident[0:TAPS, 0:TAPS])
            ins.then_inc(par_t, 1)
            for g in range(4):
                if g >= 2:
                    free_slot(g % 2, g // 2)
                for b in range(4):
                    for a in range(2):
                        c = 4 * g + b
                        ins = nc.tensor.transpose(slot[g % 2][:, b, a * P:(a + 1) * P], x_rows[:, a, c * P:(c + 1) * P],
                                                  ident[:, :])
                ins.then_inc(x_t, 1)
            statistic(stat[:, 0, :], sq_sum[:, :], sum_done, 4)

            def conv_taps(tile, t):
                pe.wait_ge(diag_done, tile + 1)
                pe.wait_ge(ulo_done, tile + 1)
                for j in range(PE_TAPS):
                    for n, (w, uu) in enumerate(((diag_hi, u_hi), (diag_hi, u_lo), (diag_lo, u_hi))):
                        ins = mm(pair_s[t][:, 0:T], w[:, t, j, :], uu[:, t, j:j + T],
                                 start=(j == 0 and n == 0), stop=(j == PE_TAPS - 1 and n == 2))
                ins.then_inc(pe_taps, 1)

            def conv_product(i, t):
                free_slot(t, U_CONV_IN // 2 + i)
                for h in range(2):
                    k = 2 * t + h
                    pe.wait_ge(lo_done, 4 * i + k + 1)
                    for kt in range(KT):
                        if isinstance(i, int) and k == 0:
                            pe.wait_ge(x_ready, kt + 1)
                        for j, (w, xx) in enumerate(((w_hi, x_hi), (w_hi, x_lo), (w_lo, x_hi))):
                            ins = mm(slot[t][:, 2 - 2 * h, :], conv_view(w[k])[:, kt, :], xx[:, kt, :],
                                     start=(kt == 0 and j == 0), stop=(kt == KT - 1 and j == 2))
                    ins.then_inc(w_used, 1)

            conv_product(0, 0)
            conv_product(0, 1)
            conv_taps(0, 0)
            with pe.Fori(1, KT // 2) as i:
                conv_product(i, 0)
                conv_taps(2 * i - 1, 1)
                conv_product(i, 1)
                conv_taps(2 * i, 0)
            conv_taps(KT - 1, 1)
            statistic(stat[:, 0, :], y_sum[:, :], ysum_done, KT + 1)
            statistic(stat[:, 1, :], sq_sum[:, :], sum_done, 8)

            def residual_product(c0, u0, x1, x2, ready, per_chunk, chunks=4):
                if chunks == RING:
                    with pe.Fori(0, 2) as i:
                        for s in range(2):
                            free_slot(s, u0 // 2 + i)
                            group(c0 + 4 * s + 8 * i, 0, s, 4, x1, x2, ready, per_chunk)
                else:
                    for g in range(4):
                        free_slot(g % 2, (u0 + g) // 2)
                        group(c0 + chunks * g, c0 + chunks * g, g % 2, chunks, x1, x2, ready, per_chunk)

            def ffn(l, x0):
                for pt, (first, pairs) in enumerate(PARTS):
                    c0, u0, h0 = C_FFN[l] + 48 * pt, U_FFN[l] + 12 * pt, HID[l] + first
                    with pe.Fori(0, pairs) as p:
                        for s in range(2):
                            free_slot(s, u0 // 2 + p)
                            group(c0 + 4 * s + 8 * p, 0, s, 4, x_hi, x_lo, (x_ready, x0))
                    residual_product(c0 + 8 * pairs, u0 + 2 * pairs, h_hi, h_lo, (hid_ready, h0), True, pairs)

            residual_product(C_CONV_OUT, U_CONV_OUT, x_hi, x_lo, (x_ready, KT), False)
            statistic(stat[:, 0, :], sq_sum[:, :], sum_done, 12)
            ffn(0, 2 * KT)
            statistic(stat[:, 0, :], sq_sum[:, :], sum_done, 16)

            pe.wait_ge(gate_in, 32)
            for k in range(KT):
                pe.wait_ge(xn_done, 3 * KT + k + 1)
                ins = mm(misc[0:RANK, 0:T], gate_w1[:, k, :], act[:, k, :], start=(k == 0), stop=(k == KT - 1))
            ins.then_inc(z1_done, 1)
            with pe.Fori(0, 2) as i:
                for s in range(2):
                    free_slot(s, U_QK // 2 + i)
                    group(C_QK + 4 * s + 8 * i, 0, s, 4, x_hi, x_lo, (x_ready, 3 * KT))
            pe.wait_ge(z1_read, 1)
            for n in range(2):
                free_slot(n, (U_GATE + n) // 2)
                for b in range(4):
                    t = 4 * n + b
                    ins = mm(slot[n][:, b, :], gate_w2[:, t * P:(t + 1) * P], gate_z1[:, :], start=True, stop=True)
                ins.then_inc(z_ready, 1)

            for a in range(2):
                for h in range(HEADS):
                    for kk in range(2):
                        tok = slice(a * P, (a + 1) * P)
                        ins = mm(pair_s[a][:, h * P:(h + 1) * P], k_t[:, 2 * h + kk, tok], q_t[:, 2 * h + kk, tok],
                                 start=(kk == 0), stop=(kk == 1))
            ins.then_inc(lev_mm, 1)

            def level_products(n):
                s = LEVELS[n]
                pe.wait_ge(lev_mul, 2 * (n + 1))
                pe.wait_ge(lev_add, 2 if n <= 1 else 3 + 2 * (n - 2))
                if n == 0:
                    for h in range(HEADS):
                        for kk in range(2):
                            ins = mm(pair_s[1][:, h * P:(h + 1) * P], dec[:, 2 * h + kk, 0:P], dec[:, 2 * h + kk, P:T],
                                     start=(kk == 0), stop=(kk == 1))
                else:
                    pr = pair_s[(n + 1) % 2]
                    for a in range(2):
                        for h in range(HEADS):
                            for kk in range(2):
                                d = dec[:, 2 * h + kk, a * P:(a + 1) * P]
                                ins = mm(pr[:, (4 * a + h) * 64:(4 * a + h + 1) * 64], d,
                                         d.rearrange("p (b h r) -> p b h r", h=2, r=s)[:, :, 1, :],
                                         start=(kk == 0), stop=(kk == 1))
                ins.then_inc(lev_mm, 1)

            for g in range(HEADS):
                free_slot(g % 2, (U_V + g) // 2)
                rows_ = slot[g % 2][:, :, :].rearrange("p (a b) t -> p a (b t)", a=2)
                for j in range(4):
                    pe.wait_ge(lo_done, C_V + 4 * g + j + 1)
                    for kt in range(4):
                        for a in range(2):
                            tok = slice(a * P, (a + 1) * P)
                            for i, (w, xx) in enumerate(((w_hi, x_hi), (w_lo, x_hi), (w_hi, x_lo))):
                                ins = mm(rows_[:, a, :], xx[:, 4 * j + kt, tok], w[j][:, kt, :],
                                         start=(j == 0 and kt == 0 and i == 0), stop=(j == 3 and kt == 3 and i == 2))
                    ins.then_inc(w_used, 1)
                    if j % 2 == 1:
                        level_products(2 * g + j // 2)
            pe.wait_ge(lev_add, 3 + 2 * 7)
            for h in range(HEADS):
                free_slot(h % 2, (U_PV + h) // 2)
                if h == 0:
                    pe.wait_ge(acc_read[1], (U_V + 3) // 2 + 1)
                for b in range(4):
                    cols = slice(h * DV + b * P, h * DV + (b + 1) * P)
                    mm(slot[h % 2][:, b, 0:P], v[:, 0, cols], s_diag[:, h, :], start=True, stop=True, skip_group_check=True)
                    mm(slot[h % 2][:, b, P:T], v[:, 0, cols], s_off[:, h, :], start=True, stop=False, skip_group_check=True)
                    ins = mm(slot[h % 2][:, b, P:T], v[:, 1, cols], s_diag[:, 4 + h, :], start=False, stop=True,
                             skip_group_check=True)
                ins.then_inc(pv_done, 1)
                if h >= 1:
                    statistic(head_stat[h - 1], head_sq[(h - 1) % 2], sum_done, 16 + h)
            statistic(head_stat[3], head_sq[1], sum_done, 20)
            with pe.Fori(0, 2) as i:
                for s in range(2):
                    free_slot(s, U_R // 2 + i)
                    group(C_R + 4 * s + 8 * i, 0, s, 4, x_hi, x_lo, (x_ready, 3 * KT))
            residual_product(C_GLA_OUT, U_GLA_OUT, h_hi, h_lo, (hid_ready, HID_GLA), True)
            statistic(stat[:, 0, :], sq_sum[:, :], sum_done, 24)
            ffn(1, 4 * KT)
            statistic(stat[:, 0, :], sq_sum[:, :], sum_done, 28)
            for a in range(2):
                for s in range(2):
                    free_slot(s, U_OUT // 2 + a)
                    for b in range(8):
                        t = 8 * s + b
                        pe.wait_ge(xn_done, 5 * KT + t + 1)
                        ins = nc.tensor.transpose(slot[s][:, b // 2, (b % 2) * P:(b % 2 + 1) * P],
                                                  act[:, t, a * P:(a + 1) * P], ident[:, :])
                    ins.then_inc(out_t, 1)


_INS = ["x", "norm_mix_g", "norm_ffn_g", "conv_w_in", "conv_b_in", "conv_w_dw", "conv_b_dw", "conv_ln_g", "conv_ln_b",
        "conv_w_out", "conv_b_out", "gla_w_in", "gla_gate_w1", "gla_gate_w2", "gla_gate_b", "gla_head_norm_g",
        "gla_w_out", "ffn_w_gate_up", "ffn_w_down", "final_norm_g"]


def kernel(**inputs):
    import numpy as _np
    import concourse.bacc as _bacc
    from concourse.bass_utils import run_bass_kernel_spmd as _run

    nc = _bacc.Bacc("TRN2", target_bir_lowering=False, num_devices=1)
    arrays, args = {}, []
    for name in _INS:
        a = _np.ascontiguousarray(inputs[name])
        arrays[f"in_{name}"] = a
        args.append(nc.dram_tensor(f"in_{name}", a.shape, mybir.dt.from_np(a.dtype), kind="ExternalInput").ap())
    args.append(nc.dram_tensor("out_0", (1, T, D), F32, kind="ExternalOutput").ap())
    trunk(nc, *args)
    r = _run(nc, [arrays], core_ids=[0])
    return r.results[0]["out_0"]
```

```python
from contextlib import ExitStack

import concourse.bass as bass
from concourse import mybir

F32 = mybir.dt.float32
F32R = mybir.dt.float32r
ALU = mybir.AluOpType
ACT = mybir.ActivationFunctionType
AX_X = mybir.AxisListType.X
ds = bass.ds

P = 128
T = 256
D = 2048
KT = D // P
FF = 5632
TAPS = 31
PAD = TAPS - 1
PE_TAPS = 4
STEPS = TAPS - PE_TAPS + 2
UW = T + PE_TAPS
HEADS = 4
DK = 256
DV = 512
RANK = 16
EPS = 1e-6
GATE_DIV = 16.0
RING = 4
AHEAD = RING - 1
GW = 512
PARTS = ((0, 4), (4, 4), (8, 3))

C_CONV_IN = 0
C_CONV_OUT = C_CONV_IN + 32
C_FFN = (C_CONV_OUT + 16, C_CONV_OUT + 16 + 132 + 64)
C_QK = C_FFN[0] + 132
C_V = C_QK + 16
C_R = C_V + 16
C_GLA_OUT = C_R + 16
C_END = C_FFN[1] + 132

U_X = 0
U_CONV_IN = U_X + 4
U_CONV_OUT = U_CONV_IN + 16
U_FFN = (U_CONV_OUT + 4, U_CONV_OUT + 4 + 34 + 20)
U_QK = U_FFN[0] + 34
U_V = U_QK + 4
U_PV = U_V + 4
U_R = U_PV + 4
U_GLA_OUT = U_R + 4
U_OUT = U_FFN[1] + 34

VECTORS = (("norm_mix", 32), ("norm_ffn", 32), ("conv_b_in", 32), ("conv_b_dw", 16), ("ln_g", 16),
           ("conv_b_out", 16), ("ln_b", 16), ("gate_b", 8), ("head_g", 16), ("final_g", 16))
VCOL = {}
_at = 0
for _name, _rows in VECTORS:
    VCOL[_name] = _at
    _at += _rows
VROWS = _at
LEVELS = (128, 64, 32, 16, 8, 4, 2, 1)
HID = (0, 11 + HEADS)
HID_GLA = 11
STAT = (1, 3, 4, 5, 6, 7, 8, 9, 10, 11)


def trunk(nc, x, norm_mix_g, norm_ffn_g, conv_w_in, conv_b_in, conv_w_dw, conv_b_dw, conv_ln_g, conv_ln_b,
          conv_w_out, conv_b_out, gla_w_in, gla_gate_w1, gla_gate_w2, gla_gate_b, gla_head_norm_g,
          gla_w_out, ffn_w_gate_up, ffn_w_down, final_norm_g, out):
    with ExitStack() as ctx:
        base = (nc.sbuf_base + 63) // 64 * 64

        def sb(name, shape, offset, dt=F32):
            return nc.alloc_sbuf_tensor_at(name, shape, dt, offset=base + offset)

        def sem(name):
            return ctx.enter_context(nc.semaphore(name))

        K = 1024
        res = sb("res", [P, KT, T], 0)
        x_hi = sb("x_hi", [P, KT, T], 16 * K, F32R)
        x_lo = sb("x_lo", [P, KT, T], 32 * K, F32R)
        act = sb("act", [P, KT, T], 48 * K)
        h_hi = sb("h_hi", [P, 16, T], 64 * K, F32R)
        h_lo = sb("h_lo", [P, 16, T], 80 * K, F32R)
        raw = [sb(f"raw{i}", [P, 4, GW], (96 + 8 * i) * K) for i in range(RING)]
        w_hi = [sb(f"w_hi{i}", [P, 4, GW], (128 + 8 * i) * K, F32R) for i in range(RING)]
        w_lo = [sb(f"w_lo{i}", [P, 4, GW], (160 + 8 * i) * K, F32R) for i in range(RING)]
        tmp = [sb(f"tmp{i}", [P, 4, T], (192 + 4 * i) * K) for i in range(2)]
        small = 200 * K
        vec = sb("vec", [P, VROWS], small)
        masks = sb("masks", [P, 7, 64], small + 832)
        ones = sb("ones", [P, P], small + 2624)
        ident = sb("ident", [P, P], small + 3136)
        rstd = sb("rstd", [P, T], small + 3648)
        sq_part = sb("sq_part", [P, T], small + 4672)
        sq_sum = sb("sq_sum", [P, T], small + 5696)
        eps = sb("eps", [P, 1], small + 6720)
        rstd_tok = sb("rstd_tok", [P, 2], small + 6752)
        assert base + small + 6784 <= nc.sbuf_usable_end

        x_rows = sb("x_rows", [P, 2, D], 64 * K)
        vec_rows = sb("vec_rows", [P, 2, P], 80 * K)
        dw_rows = sb("dw_rows", [TAPS, D], 81 * K)
        dw = sb("dw", [P, KT * TAPS], 89 * K)
        u = sb("u", [P, 2, PAD + T], 64 * K)
        gate = sb("gate", [P, 2, T], 67 * K)
        y_odd = sb("y_odd", [P, T], 78 * K)
        u_hi = sb("u_hi", [P, 2, UW], 73 * K + 512, F32R)
        u_lo = sb("u_lo", [P, 2, UW], 75 * K + 768, F32R)
        diag_hi = sb("diag_hi", [P, 2, PE_TAPS, P], 80 * K, F32R)
        diag_lo = sb("diag_lo", [P, 2, PE_TAPS, P], 84 * K, F32R)
        dw_hi = sb("dw_hi", [P, KT * TAPS], 91 * K, F32R)
        dw_lo = sb("dw_lo", [P, KT * TAPS], 93 * K)
        y_sum = sb("y_sum", [P, T], 69 * K)
        ln_sq = sb("ln_sq", [P, 2, 4, T], 32 * K)
        v = sb("v", [P, 2, D], 64 * K)
        cum = sb("cum", [P, 8, T], 80 * K)
        dec = sb("dec", [P, 8, T], 88 * K)
        o_sq = sb("o_sq", [P, HEADS, 4, T], 80 * K)
        gate_w1 = sb("gate_w1", [P, KT, RANK], 76 * K)
        gate_w1_hi = sb("gate_w1_hi", [P, KT, RANK], 77 * K, F32R)
        gate_w1_lo = sb("gate_w1_lo", [P, KT, RANK], 78 * K, F32R)
        gate_z1 = sb("gate_z1", [RANK, T], 79 * K)
        gate_w2 = sb("gate_w2", [RANK, HEADS * DK], 92 * K)
        s_diag = sb("s_diag", [P, 2 * HEADS, P], 192 * K)
        s_off = sb("s_off", [P, HEADS, P], 196 * K)
        q_t = act[:, 0:8, :]
        k_t = act[:, 8:16, :]
        out_rows = sb("out_rows", [P, 2, D], 64 * K)

        slot = [ctx.enter_context(nc.psum_tensor(f"slot{i}", [P, 4, T], F32)) for i in range(2)]
        stat = ctx.enter_context(nc.psum_tensor("stat", [P, 2, T], F32))
        pair_s = [ctx.enter_context(nc.psum_tensor(f"pair_s{i}", [P, 512], F32)) for i in range(2)]
        misc = ctx.enter_context(nc.psum_tensor("misc", [P, 512], F32))

        raw_in = [sem(f"raw_in{i}") for i in range(RING)]
        hi_done = sem("hi_done")
        lo_done = sem("lo_done")
        w_used = sem("w_used")
        acc_read = [sem(f"acc_read{i}") for i in range(2)]
        rows_in = sem("rows_in")
        gate_in = sem("gate_in")
        consts = sem("consts")
        gate_split = sem("gate_split")
        par_t = sem("par_t")
        par_read = sem("par_read")
        x_t = sem("x_t")
        sq_done = sem("sq_done")
        sum_done = sem("sum_done")
        stat_done = sem("stat_done")
        root_done = sem("root_done")
        rstd_done = sem("rstd_done")
        xn_done = sem("xn_done")
        xhi_done = sem("xhi_done")
        x_ready = sem("x_ready")
        sig_done = sem("sig_done")
        tap_done = sem("tap_done")
        uhi_done = sem("uhi_done")
        ulo_done = sem("ulo_done")
        diag_done = sem("diag_done")
        pe_taps = sem("pe_taps")
        dw_split = sem("dw_split")
        ysum_done = sem("ysum_done")
        part_done = sem("part_done")
        mean_done = sem("mean_done")
        cent_done = sem("cent_done")
        z_done = sem("z_done")
        hid_hi = sem("hid_hi")
        hid_ready = sem("hid_ready")
        silu_done = sem("silu_done")
        up_scaled = sem("up_scaled")
        z1_done = sem("z1_done")
        z1_read = sem("z1_read")
        z_ready = sem("z_ready")
        z_read = sem("z_read")
        ls_act = sem("ls_act")
        ls_vec = sem("ls_vec")
        lev_diff = sem("lev_diff")
        lev_exp = sem("lev_exp")
        lev_mul = sem("lev_mul")
        lev_mm = sem("lev_mm")
        lev_add = sem("lev_add")
        pv_done = sem("pv_done")
        o_norm = sem("o_norm")
        out_t = sem("out_t")
        rows_out = [sem(f"rows_out{a}") for a in range(2)]
        stored = sem("stored")

        block = ctx.enter_context(nc.Block())

        conv_in_w = conv_w_in[0].rearrange("(k p) n -> p k n", p=P)
        conv_out_w = conv_w_out[0].rearrange("(k p) n -> p k n", p=P)
        gla_in_w = gla_w_in[0].rearrange("(k p) n -> p k n", p=P)
        gla_out_w = gla_w_out[0].rearrange("(k p) n -> p k n", p=P)
        up_w = [ffn_w_gate_up[i].rearrange("(k p) n -> p k n", p=P) for i in range(2)]
        down_w = [ffn_w_down[i].rearrange("(k p) n -> p k n", p=P) for i in range(2)]

        def conv_view(tile):
            return tile[:, :, :].rearrange("p a (b c) -> p (a b) c", c=P)

        def over(row, n):
            return row.unsqueeze(1).broadcast_to([P, n, row.shape[1]])

        head_sq = [sq_sum[:, :], sq_part[:, :], tmp[1][:, 2, :], tmp[1][:, 3, :]]
        head_rstd = [o_sq[:, h, 0, :] for h in range(HEADS)]
        z_bank = [pair_s[0][:, :], pair_s[1][:, :], misc[:, :], stat[:, :, :].rearrange("p a t -> p (a t)")]
        out_bank = [[slot[0][:, 2 * a:2 * a + 2, :].rearrange("p b t -> p (b t)") for a in range(2)],
                    z_bank[0:2], z_bank[2:4],
                    [slot[1][:, 2 * a:2 * a + 2, :].rearrange("p b t -> p (b t)") for a in range(2)]]
        head_stat = [stat[:, 0, :], misc[:, 0:T], pair_s[0][:, 0:T], pair_s[1][:, 0:T]]

        def vcol(name, i):
            return vec[:, VCOL[name] + i:VCOL[name] + i + 1]

        @block.sync
        def _(sp):
            def rows(dst, src):
                sp.dma_start(dst, src).then_inc(rows_in, 16)

            def load(c, k, dst, src, first=False):
                if not first:
                    sp.wait_ge(lo_done, c - RING + 1)
                sp.dma_start(dst, src).then_inc(raw_in[k], 16)

            def matrix(c0, w, col0, groups, chunks=4, k0=0):
                per = 1 if chunks == RING else groups
                with sp.Fori(0, groups // per) as g:
                    for j in range(per * chunks):
                        load(c0 + per * chunks * g + j, j % RING, raw[j % RING][:, :, :],
                             w[:, k0 + 4 * (j % chunks):k0 + 4 * (j % chunks) + 4,
                               ds(col0 + GW * (g * per + j // chunks), GW)])

            rows(x_rows[:, :, :], x[0].rearrange("(a p) d -> p a d", p=P))
            at = 0
            for name, src in (("norm_mix", norm_mix_g), ("norm_ffn", norm_ffn_g), ("conv_b_in", conv_b_in),
                              ("conv_b_dw", conv_b_dw), ("ln_g", conv_ln_g)):
                n = dict(VECTORS)[name]
                rows(vec_rows[at:at + n, 0, :], src.rearrange("a (r c) -> (a r) c", c=P))
                at += n
            assert at == P
            at = 0
            for name, src in (("conv_b_out", conv_b_out), ("ln_b", conv_ln_b), ("gate_b", gla_gate_b),
                              ("head_g", gla_head_norm_g[0]), ("final_g", final_norm_g.rearrange("(a d) -> a d", a=1))):
                n = dict(VECTORS)[name]
                rows(vec_rows[at:at + n, 1, :], src.rearrange("a (r c) -> (a r) c", c=P))
                at += n
            rows(dw_rows[:, :], conv_w_dw[0])

            def conv_turn(i, i0, first):
                for t in range(2):
                    for h in range(2):
                        k = 2 * t + h
                        src = conv_in_w[:, :, ds(2 * P * i + (2 * P * i0 + P * t + D * (1 - h)), P)]
                        load(4 * i + (4 * i0 + k), k, conv_view(raw[k]), src, first)

            conv_turn(0, 0, True)
            with sp.Fori(0, KT // 2 - 1) as i:
                conv_turn(i, 1, False)
            matrix(C_CONV_OUT, conv_out_w, 0, 4)

            def ffn(l):
                for pt, (first, pairs) in enumerate(PARTS):
                    c0 = C_FFN[l] + 48 * pt
                    with sp.Fori(0, pairs) as p:
                        for half in range(2):
                            for j in range(4):
                                load(c0 + 8 * p + 4 * half + j, j, raw[j][:, :, :],
                                     up_w[l][:, 4 * j:4 * j + 4, ds(half * FF + GW * first + GW * p, GW)])
                    matrix(c0 + 8 * pairs, down_w[l], 0, 4, chunks=pairs, k0=4 * first)

            ffn(0)
            matrix(C_QK, gla_in_w, 0, 12)
            matrix(C_GLA_OUT, gla_out_w, 0, 4)
            ffn(1)

            for n in range(2):
                for a in range(2):
                    sp.wait_ge(rows_out[a], 2 * n + 2)
                    cols = slice(2 * n * GW, (2 * n + 2) * GW)
                    sp.dma_start(out[0, a * P:(a + 1) * P, cols], out_rows[:, a, cols]).then_inc(stored, 16)
            sp.wait_ge(stored, 64)

        @block.gpsimd
        def _(pool):
            def lo(c, k, wait_order=False):
                if wait_order:
                    pool.wait_ge(lo_done, c)
                pool.wait_ge(hi_done, c + 1)
                nc.gpsimd.tensor_tensor(w_lo[k][:, :, :], raw[k][:, :, :], w_hi[k][:, :, :].bitcast(F32),
                                        ALU.subtract).then_inc(lo_done, 1)

            nc.gpsimd.memset(ident[:, :], 0.0).then_inc(consts, 1)
            nc.gpsimd.memset(ones[:, :], 1.0).then_inc(consts, 1)
            nc.gpsimd.memset(eps[:, :], EPS).then_inc(consts, 1)
            nc.gpsimd.memset(masks[:, :, :], 1.0).then_inc(consts, 1)
            pool.wait_ge(consts, 4)
            nc.gpsimd.affine_select(out=ident[:, :], in_=ident[:, :], compare_op=ALU.not_equal, fill=1.0,
                                    base=0, pattern=[[-1, P]], channel_multiplier=1).then_inc(consts, 1)
            n = 5
            for m, s in enumerate(LEVELS[1:]):
                v3 = masks[:, m, :].rearrange("p (b r) -> p b r", r=s)
                nc.gpsimd.affine_select(out=v3, in_=v3, compare_op=ALU.is_ge, fill=0.0, base=0,
                                        pattern=[[-2 * s, 64 // s], [0, s]], channel_multiplier=1).then_inc(consts, 1)
                n += 1
                pool.wait_ge(consts, n)
                nc.gpsimd.affine_select(out=v3, in_=v3, compare_op=ALU.is_ge, fill=0.0, base=s - 1,
                                        pattern=[[2 * s, 64 // s], [0, s]], channel_multiplier=-1).then_inc(consts, 1)
                n += 1
            for c in range(AHEAD):
                lo(c, c)
            def lo_turn(i):
                for j in range(AHEAD, AHEAD + 4):
                    lo(4 * i + j, j % RING)

            def sum_y(tile, done):
                pool.wait_ge(tap_done, done)
                pool.wait_ge(ysum_done, tile + 1)
                nc.gpsimd.tensor_tensor(y_sum[:, :], y_sum[:, :], act[:, ds(tile, 1), :].rearrange("p a t -> p (a t)"),
                                        ALU.add).then_inc(ysum_done, 1)

            lo_turn(0)
            with pool.Fori(0, KT // 2 - 1) as i:
                for t in range(2):
                    for h in range(2):
                        j = 2 * t + h + AHEAD
                        lo(4 * i + (4 + j), j % RING)
                    sum_y(2 * i + t, 2 * STEPS * i + (STEPS * (t + 1) + 2))
            for t in range(KT - 2, KT):
                sum_y(t, STEPS * (t + 1) + 2)
            pool.wait_ge(w_used, C_FFN[0] + 96)
            pool.dma_start(gate_w1[:, :, :], gla_gate_w1[0].rearrange("(k p) r -> p k r", p=P)).then_inc(gate_in, 16)
            pool.dma_start(gate_w2[:, :], gla_gate_w2[0]).then_inc(gate_in, 16)
            pool.wait_ge(gate_split, 1)
            nc.gpsimd.tensor_tensor(gate_w1_lo[:, :, :], gate_w1[:, :, :], gate_w1_hi[:, :, :].bitcast(F32),
                                    ALU.subtract).then_inc(gate_split, 1)
            for j in range(16):
                lo(C_V + AHEAD + j, (AHEAD + j) % RING, wait_order=(j == 0))

        @block.scalar
        def _(scalar):
            def hi(c4, k):
                scalar.wait_ge(raw_in[k], 16 * c4 + 16)
                if not (isinstance(c4, int) and c4 == 0):
                    scalar.wait_ge(w_used, 4 * c4 + k - RING + 1)
                nc.scalar.activation(w_hi[k][:, :, :], raw[k][:, :, :], ACT.Copy).then_inc(hi_done, 1)

            def hi_group(c0, chunks=4):
                for c in range(c0 + AHEAD, min(c0 + AHEAD + chunks, C_END)):
                    hi(c // RING, c % RING)

            def hi_group_at(c4):
                for j in range(AHEAD, AHEAD + 4):
                    hi(c4 + j // RING, j % RING)

            def root(n, to, src, scale):
                scalar.wait_ge(stat_done, STAT[n])
                nc.scalar.activation(to, src, ACT.Sqrt, bias=eps[:, 0:1], scale=scale).then_inc(root_done, 1)

            def split_tiles(n):
                for t in range(KT):
                    scalar.wait_ge(xn_done, n + t + 1)
                    nc.scalar.activation(x_hi[:, t, :], act[:, t, :], ACT.Copy).then_inc(xhi_done, 1)

            def squares(use0, n0, g):
                scalar.wait_ge(acc_read[g % 2], (use0 + g) // 2 + 1)
                if g >= 2:
                    scalar.wait_ge(sum_done, n0 + g - 1)
                nc.scalar.activation(tmp[g % 2][:, :, :], res[:, 4 * g:4 * g + 4, :], ACT.Square).then_inc(sq_done, 1)

            def gains(to, signal, name, v0, g):
                for t in range(4 * g, 4 * g + 4):
                    nc.scalar.activation(to[:, t, :], res[:, t, :], ACT.Copy, scale=vcol(name, v0 + t)).then_inc(signal, 1)

            for g in range(4):
                squares(U_X, 0, g)
            for c in range(AHEAD):
                hi(0, c)
            root(0, rstd[:, :], stat[:, 0, :], 1.0 / D)
            split_tiles(0)

            def diagonals(tile, t):
                for j in range(PE_TAPS):
                    for parts, weights in ((diag_hi, dw), (diag_lo, dw_lo)):
                        ins = nc.scalar.activation(parts[:, t, j, :], ident[:, :], ACT.Copy,
                                                   scale=weights[:, ds(TAPS * tile + j, 1)])
                ins.then_inc(diag_done, 1)

            def conv_turn(i):
                for t in range(2):
                    j = 2 * t + AHEAD
                    hi(i + j // RING, j % RING)
                    scalar.wait_ge(w_used, 4 * i + 2 * t + 1)
                    scalar.wait_ge(acc_read[t], U_CONV_IN // 2 + i)
                    nc.scalar.activation(gate[:, t, :], slot[t][:, 2, :], ACT.Sigmoid,
                                         bias=vec[:, ds(VCOL["conv_b_in"] + KT + t + 2 * i, 1)]).then_inc(sig_done, 1)
                    if not (isinstance(i, int) and i == 0):
                        scalar.wait_ge(pe_taps, 2 * i + t - 1)
                    diagonals(2 * i + t, t)
                    hi(i + (j + 1) // RING, (j + 1) % RING)
                    scalar.wait_ge(acc_read[t], U_CONV_IN // 2 + 1 + i)
                    nc.scalar.activation(u_hi[:, t, :], u[:, t, 0:UW], ACT.Copy).then_inc(uhi_done, 1)

            scalar.wait_ge(par_read, 2)
            nc.scalar.activation(dw_hi[:, :], dw[:, :], ACT.Copy).then_inc(dw_split, 1)
            scalar.wait_ge(dw_split, 2)
            conv_turn(0)
            with scalar.Fori(1, KT // 2) as i:
                conv_turn(i)
            for g in range(4):
                scalar.wait_ge(cent_done, g + 1)
                if g >= 2:
                    scalar.wait_ge(sum_done, 4 + g - 1)
                nc.scalar.activation(ln_sq[:, g % 2, :, :], act[:, 4 * g:4 * g + 4, :], ACT.Square).then_inc(sq_done, 1)
            root(1, rstd[:, :], stat[:, 1, :], 1.0 / D)
            for t in range(KT):
                if t % 4 == 0:
                    scalar.wait_ge(z_done, t // 4 + 1)
                nc.scalar.activation(act[:, t, :], act[:, t, :], ACT.Silu, bias=vcol("ln_b", t),
                                     scale=vcol("ln_g", t)).then_inc(xn_done, 1)
                scalar.wait_ge(xn_done, KT + t + 1)
                nc.scalar.activation(h_hi[:, t, :], act[:, t, :], ACT.Copy).then_inc(xhi_done, 1)
            for g in range(4):
                hi_group(C_CONV_OUT + 4 * g)
                squares(U_CONV_OUT, 8, g)
                gains(x_hi, xhi_done, "norm_ffn", 0, g)

            def ffn(l, n_sq, n_root, gain):
                for pt, (first, pairs) in enumerate(PARTS):
                    c0, u0 = C_FFN[l] + 48 * pt, U_FFN[l] + 12 * pt
                    def pair(p, with_root=False):
                        hi_group_at(c0 // 4 + 2 * p)
                        if with_root:
                            root(n_root, rstd[:, :], stat[:, 0, :], 1.0 / D)
                        scalar.wait_ge(acc_read[0], u0 // 2 + p + 1)
                        nc.scalar.activation(tmp[0][:, :, :], tmp[0][:, :, :], ACT.Silu).then_inc(silu_done, 1)
                        hi_group_at(c0 // 4 + 1 + 2 * p)
                        scalar.wait_ge(acc_read[1], u0 // 2 + p + 1)
                        nc.scalar.activation(h_hi[:, ds(4 * p, 4), :], tmp[1][:, :, :], ACT.Copy).then_inc(hid_hi, 1)

                    if pt == 0:
                        pair(0, True)
                    with scalar.Fori(1 if pt == 0 else 0, pairs) as p:
                        pair(p)
                    d0, du = c0 + 8 * pairs, u0 + 2 * pairs
                    if pt < 2:
                        with scalar.Fori(0, 4) as g:
                            hi_group_at(d0 // 4 + g)
                    else:
                        for g in range(4):
                            hi_group(d0 + pairs * g, pairs)
                            squares(du, n_sq, g)
                            gain(g)
                            if l == 0 and g == 0:
                                scalar.wait_ge(gate_in, 32)
                                nc.scalar.activation(gate_w1_hi[:, :, :], gate_w1[:, :, :], ACT.Copy).then_inc(gate_split, 1)

            ffn(0, 12, 2, lambda g: gains(x_hi, xhi_done, "norm_mix", KT, g))

            hi_group(C_QK)
            root(3, rstd[:, :], stat[:, 0, :], 1.0 / D)
            hi_group(C_QK + 4)
            hi_group(C_QK + 8, 1)
            scalar.wait_ge(z_read, 4)
            nc.scalar.activation(dec[:, :, :], cum[:, :, :], ACT.Abs).then_inc(ls_act, 1)
            scalar.wait_ge(ls_act, 1)
            nc.scalar.activation(dec[:, :, :], dec[:, :, :], ACT.Exp, scale=-1.0).then_inc(ls_act, 1)
            hi_group(C_QK + 9, 1)
            scalar.wait_ge(ls_act, 2)
            nc.scalar.activation(dec[:, :, :], dec[:, :, :], ACT.Ln, bias=1.0).then_inc(ls_act, 1)
            hi_group(C_QK + 10, 6)

            def level_exp(n):
                scalar.wait_ge(lev_diff, 2 * (n + 1))
                nc.scalar.activation(dec[:, :, :], dec[:, :, :], ACT.Exp, scale=1.0 / GATE_DIV).then_inc(lev_exp, 1)

            for g in range(4):
                for j in range(4):
                    c = C_V + 4 * g + j + AHEAD
                    hi(c // RING, c % RING)
                    if j % 2 == 0:
                        level_exp(2 * g + j // 2)
                scalar.wait_ge(w_used, C_V + 4 * g + 4)
                if g == 0:
                    scalar.wait_ge(z1_read, 2)
                for a in range(2):
                    ins = nc.scalar.activation(v[:, a, g * DV:(g + 1) * DV],
                                               slot[g % 2][:, 2 * a:2 * a + 2, :].rearrange("p b t -> p (b t)"),
                                               ACT.Copy, scale=rstd_tok[:, a:a + 1])
                ins.then_inc(acc_read[g % 2], 1)
            scalar.wait_ge(lev_mm, len(LEVELS) + 1)
            for h in range(HEADS):
                scalar.wait_ge(acc_read[h % 2], (U_PV + h) // 2 + 1)
                nc.scalar.activation(o_sq[:, h, :, :], act[:, 4 * h:4 * h + 4, :], ACT.Square).then_inc(sq_done, 1)
            for h in range(HEADS):
                hi_group(C_R + 4 * h)
                if h == 0:
                    for n in range(HEADS):
                        root(4 + n, head_rstd[n], head_stat[n], 1.0 / DV)
                scalar.wait_ge(acc_read[h % 2], (U_R + h) // 2 + 1)
                nc.scalar.activation(tmp[0][:, :, :], tmp[0][:, :, :], ACT.Silu).then_inc(silu_done, 1)
                scalar.wait_ge(z_done, 4 + h + 1)
                nc.scalar.activation(h_hi[:, 4 * h:4 * h + 4, :], tmp[1][:, :, :], ACT.Copy).then_inc(hid_hi, 1)
            for g in range(4):
                hi_group(C_GLA_OUT + 4 * g)
                squares(U_GLA_OUT, 20, g)
                gains(x_hi, xhi_done, "norm_ffn", KT, g)
            ffn(1, 24, 8, lambda g: gains(act, xn_done, "final_g", 0, g))
            root(9, rstd_tok[:, :], stat[:, 0, 0:2], 1.0 / D)
            scalar.wait_ge(rstd_done, 10)
            for g, part in ((0, 1), (1, 2), (3, 4), (2, 5)):
                scalar.wait_ge(out_t, part)
                nc.scalar.activation(out_rows[:, 1, g * GW:(g + 1) * GW], out_bank[g][1], ACT.Copy,
                                     scale=rstd_tok[:, 1:2]).then_inc(rows_out[1], 1)

        @block.vector
        def _(dve):
            def lo(c, k, wait_order=False):
                if wait_order:
                    dve.wait_ge(lo_done, c)
                dve.wait_ge(hi_done, c + 1)
                nc.vector.tensor_tensor(w_lo[k][:, :, :], raw[k][:, :, :], w_hi[k][:, :, :].bitcast(F32),
                                        ALU.subtract).then_inc(lo_done, 1)

            def lo_group(c0, chunks=4, wait_order=False):
                for j in range(chunks):
                    c = c0 + AHEAD + j
                    if c < C_END:
                        lo(c, c % RING, wait_order and j == 0)

            def lo_group_at(c0, g, step):
                for j in range(4):
                    lo(c0 + AHEAD + j + step * g, (AHEAD + j) % RING)

            def sum_squares(n0, g, src):
                dve.wait_ge(sq_done, n0 + g + 1)
                if g == 0:
                    nc.vector.tensor_reduce(sq_sum[:, :], src.rearrange("p k t -> p t k"), AX_X, ALU.add).then_inc(sum_done, 1)
                    return
                dve.wait_ge(sum_done, n0 + g)
                nc.vector.tensor_reduce(sq_part[:, :], src.rearrange("p k t -> p t k"), AX_X, ALU.add).then_inc(part_done, 1)
                parts[0] += 1
                dve.wait_ge(part_done, parts[0])
                nc.vector.tensor_tensor(sq_sum[:, :], sq_sum[:, :], sq_part[:, :], ALU.add).then_inc(sum_done, 1)

            def invert(n, buf):
                dve.wait_ge(root_done, n + 1)
                nc.vector.reciprocal(buf, buf).then_inc(rstd_done, 1)
                dve.wait_ge(rstd_done, n + 1)

            def rms_tiles(name, v0, n):
                def remainder(t):
                    dve.wait_ge(xhi_done, n + t + 1)
                    nc.vector.tensor_tensor(x_lo[:, t, :], act[:, t, :], x_hi[:, t, :].bitcast(F32),
                                            ALU.subtract).then_inc(x_ready, 1)

                for t in range(KT):
                    nc.vector.scalar_tensor_tensor(out=act[:, t, :], in0=res[:, t, :], scalar=vcol(name, v0 + t),
                                                   in1=rstd[:, :], op0=ALU.mult, op1=ALU.mult).then_inc(xn_done, 1)
                    if t >= 1:
                        remainder(t - 1)
                remainder(KT - 1)

            def gain_remainders(name, v0, n, g):
                for t in range(4 * g, 4 * g + 4):
                    dve.wait_ge(xhi_done, n + t + 1)
                    nc.vector.scalar_tensor_tensor(out=x_lo[:, t, :], in0=res[:, t, :], scalar=vcol(name, v0 + t),
                                                   in1=x_hi[:, t, :].bitcast(F32), op0=ALU.mult,
                                                   op1=ALU.subtract).then_inc(x_ready, 1)

            parts = [0]

            dve.wait_ge(par_t, 1)
            nc.vector.tensor_copy(vec[:, :], misc[:, 0:VROWS]).then_inc(par_read, 1)
            dve.wait_ge(par_t, 2)
            nc.vector.tensor_copy(dw[:, :], pair_s[0][:, 0:KT * TAPS]).then_inc(par_read, 1)
            for g in range(4):
                dve.wait_ge(x_t, g + 1)
                nc.vector.tensor_copy(res[:, 4 * g:4 * g + 4, :], slot[g % 2][:, :, :]).then_inc(acc_read[g % 2], 1)
                if g >= 1:
                    sum_squares(0, g - 1, tmp[(g - 1) % 2][:, :, :])
            sum_squares(0, 3, tmp[1][:, :, :])
            invert(0, rstd[:, :])
            rms_tiles("norm_mix", 0, 0)

            dve.wait_ge(x_t, 4)
            nc.vector.memset(y_sum[:, :], 0.0).then_inc(ysum_done, 1)
            nc.vector.memset(u[:, 0, 0:PAD], 0.0).then_inc(tap_done, 1)
            nc.vector.memset(u[:, 1, 0:PAD], 0.0).then_inc(tap_done, 1)
            def conv_tile(i, t):
                y = act[:, ds(2 * i + t, 1), :].rearrange("p a t -> p (a t)")
                done = STEPS * t + 2 + 2 * STEPS * i
                dve.wait_ge(sig_done, 2 * i + t + 1)
                dve.wait_ge(w_used, 4 * i + 2 * t + 2)
                dve.wait_ge(tap_done, done)
                if not (isinstance(i, int) and i == 0):
                    dve.wait_ge(uhi_done, 2 * i + t - 1)
                nc.vector.scalar_tensor_tensor(out=u[:, t, PAD:PAD + T], in0=slot[t][:, 0, :],
                                               scalar=vec[:, ds(VCOL["conv_b_in"] + t + 2 * i, 1)],
                                               in1=gate[:, t, :], op0=ALU.add, op1=ALU.mult).then_inc(acc_read[t], 1)
                dve.wait_ge(acc_read[t], U_CONV_IN // 2 + i + 1)
                for n, j in enumerate(range(PE_TAPS, TAPS)):
                    acc = (y, y_odd[:, :])[n % 2]
                    w = dw[:, ds(TAPS * (2 * i + t) + j, 1)]
                    if n == 0:
                        nc.vector.tensor_scalar(acc, u[:, t, j:j + T], w, vec[:, ds(VCOL["conv_b_dw"] + t + 2 * i, 1)],
                                                ALU.mult, ALU.add).then_inc(tap_done, 1)
                    elif n == 1:
                        nc.vector.tensor_scalar(acc, u[:, t, j:j + T], w, None, ALU.mult).then_inc(tap_done, 1)
                    else:
                        dve.wait_ge(tap_done, done + n - 1)
                        nc.vector.scalar_tensor_tensor(out=acc, in0=u[:, t, j:j + T], scalar=w, in1=acc,
                                                       op0=ALU.mult, op1=ALU.add).then_inc(tap_done, 1)
                    if n == 2:
                        dve.wait_ge(uhi_done, 2 * i + t + 1)
                        nc.vector.tensor_tensor(u_lo[:, t, :], u[:, t, 0:UW], u_hi[:, t, :].bitcast(F32),
                                                ALU.subtract).then_inc(ulo_done, 1)
                dve.wait_ge(pe_taps, 2 * i + t + 1)
                early = (y, y_odd[:, :])[(STEPS - 3 + 1) % 2]
                dve.wait_ge(tap_done, done + STEPS - 3)
                nc.vector.tensor_tensor(early, pair_s[t][:, 0:T], early, ALU.add).then_inc(tap_done, 1)
                dve.wait_ge(tap_done, done + STEPS - 1)
                nc.vector.tensor_tensor(y, y, y_odd[:, :], ALU.add).then_inc(tap_done, 1)

            dve.wait_ge(dw_split, 1)
            nc.vector.tensor_tensor(dw_lo[:, :], dw[:, :], dw_hi[:, :].bitcast(F32), ALU.subtract).then_inc(dw_split, 1)
            for t in range(2):
                conv_tile(0, t)
            with dve.Fori(1, KT // 2) as i:
                for t in range(2):
                    conv_tile(i, t)

            dve.wait_ge(stat_done, STAT[1] - 1)
            nc.vector.tensor_scalar(rstd[:, :], stat[:, 0, :], 1.0 / D, None, ALU.mult).then_inc(mean_done, 1)
            dve.wait_ge(mean_done, 1)
            for g in range(4):
                nc.vector.tensor_tensor(act[:, 4 * g:4 * g + 4, :], act[:, 4 * g:4 * g + 4, :], over(rstd[:, :], 4),
                                        ALU.subtract).then_inc(cent_done, 1)
                if g >= 1:
                    sum_squares(4, g - 1, ln_sq[:, (g - 1) % 2, :, :])
            sum_squares(4, 3, ln_sq[:, 1, :, :])
            invert(1, rstd[:, :])

            def ln_remainder(t):
                dve.wait_ge(xhi_done, KT + t + 1)
                nc.vector.tensor_tensor(h_lo[:, t, :], act[:, t, :], h_hi[:, t, :].bitcast(F32),
                                        ALU.subtract).then_inc(x_ready, 1)
            for g in range(4):
                nc.vector.tensor_tensor(act[:, 4 * g:4 * g + 4, :], act[:, 4 * g:4 * g + 4, :], over(rstd[:, :], 4),
                                        ALU.mult).then_inc(z_done, 1)
                if g >= 1:
                    for t in range(4 * g - 4, 4 * g):
                        ln_remainder(t)
            for t in range(12, 16):
                ln_remainder(t)

            def residual_group(c_end, use, g, bias=None):
                dve.wait_ge(w_used, c_end + 1)
                if bias is None:
                    nc.vector.tensor_tensor(res[:, ds(4 * g, 4), :], slot[use % 2][:, :, :], res[:, ds(4 * g, 4), :],
                                            ALU.add).then_inc(acc_read[use % 2], 1)
                    return
                for b in range(4):
                    ins = nc.vector.scalar_tensor_tensor(out=res[:, 4 * g + b, :], in0=slot[use % 2][:, b, :],
                                                         scalar=vcol(bias, 4 * g + b), in1=res[:, 4 * g + b, :],
                                                         op0=ALU.add, op1=ALU.add)
                ins.then_inc(acc_read[use % 2], 1)

            def residual_and_squares(c0, use0, n0, gains, chunks=4, bias=None, order=False):
                for g in range(4):
                    lo_group(c0 + chunks * g, chunks, wait_order=order and g == 0)
                    residual_group(c0 + chunks * (g + 1) - 1, use0 + g, g, bias)
                    if g >= 1:
                        sum_squares(n0, g - 1, tmp[(g - 1) % 2][:, :, :])
                        if gains:
                            gain_remainders(*gains, g - 1)
                sum_squares(n0, 3, tmp[1][:, :, :])
                if gains:
                    gain_remainders(*gains, 3)

            residual_and_squares(C_CONV_OUT, U_CONV_OUT, 8, ("norm_ffn", 0, 2 * KT), bias="conv_b_out", order=True)

            def ffn(l, n_sq, n_root, gains):
                for pt, (first, pairs) in enumerate(PARTS):
                    c0, u0, h0 = C_FFN[l] + 48 * pt, U_FFN[l] + 12 * pt, HID[l] + first
                    def pair(p, with_root=False):
                        lo_group_at(c0, p, 8)
                        if with_root:
                            invert(n_root, rstd[:, :])
                        dve.wait_ge(w_used, c0 + 8 * p + 4)
                        dve.wait_ge(acc_read[1], u0 // 2 + p)
                        nc.vector.tensor_tensor(tmp[0][:, :, :], slot[0][:, :, :], over(rstd[:, :], 4),
                                                ALU.mult).then_inc(acc_read[0], 1)
                        lo_group_at(c0 + 4, p, 8)
                        dve.wait_ge(silu_done, h0 + p + 1)
                        nc.vector.tensor_tensor(tmp[0][:, :, :], tmp[0][:, :, :], over(rstd[:, :], 4),
                                                ALU.mult).then_inc(up_scaled, 1)
                        dve.wait_ge(up_scaled, 11 * l + first + p + 1)
                        dve.wait_ge(w_used, c0 + 8 * p + 8)
                        nc.vector.tensor_tensor(tmp[1][:, :, :], slot[1][:, :, :], tmp[0][:, :, :],
                                                ALU.mult).then_inc(acc_read[1], 1)
                        dve.wait_ge(hid_hi, h0 + p + 1)
                        nc.vector.tensor_tensor(h_lo[:, ds(4 * p, 4), :], tmp[1][:, :, :],
                                                h_hi[:, ds(4 * p, 4), :].bitcast(F32), ALU.subtract).then_inc(hid_ready, 1)

                    if pt == 0:
                        pair(0, True)
                    with dve.Fori(1 if pt == 0 else 0, pairs) as p:
                        pair(p)
                    d0, du = c0 + 8 * pairs, u0 + 2 * pairs
                    if pt < 2:
                        with dve.Fori(0, 2) as i:
                            for g in range(2):
                                lo_group_at(d0 + 4 * g, i, 8)
                                residual_group(d0 + 4 * g + 3 + 8 * i, g, 2 * i + g)
                    else:
                        residual_and_squares(d0, du, n_sq, gains, chunks=pairs)

            ffn(0, 12, 2, ("norm_mix", KT, 3 * KT))

            def qk_group(g):
                dve.wait_ge(w_used, C_QK + 4 * g + 4)
                nc.vector.scalar_tensor_tensor(out=act[:, 4 * g:4 * g + 4, :], in0=slot[g % 2][:, :, :],
                                               scalar=DK ** -0.5 if g < 2 else 1.0, in1=over(rstd[:, :], 4),
                                               op0=ALU.mult, op1=ALU.mult).then_inc(acc_read[g % 2], 1)

            lo_group(C_QK)
            invert(3, rstd[:, :])
            qk_group(0)
            dve.wait_ge(z1_done, 1)
            nc.vector.tensor_tensor(gate_z1[:, :], misc[0:RANK, 0:T], rstd[0:RANK, :], ALU.mult).then_inc(z1_read, 1)
            nc.vector.tensor_copy(rstd_tok[:, :], misc[:, T:T + 2]).then_inc(z1_read, 1)
            lo_group(C_QK + 4)
            qk_group(1)
            for n in range(4):
                dve.wait_ge(z_ready, n + 1)
                for b in range(2):
                    ins = nc.vector.tensor_scalar(cum[:, 2 * n + b, :], z_bank[n][:, b * T:(b + 1) * T],
                                                  vcol("gate_b", 2 * n + b), None, ALU.add)
                ins.then_inc(z_read, 1)
            lo_group(C_QK + 8)
            nc.vector.memset(sq_part[:, :], 1.0).then_inc(ls_vec, 1)
            dve.wait_ge(ls_act, 3)
            nc.vector.scalar_tensor_tensor(out=cum[:, :, :], in0=cum[:, :, :], scalar=0.0, in1=dec[:, :, :],
                                           op0=ALU.min, op1=ALU.subtract).then_inc(ls_vec, 1)
            dve.wait_ge(ls_vec, 2)
            for t in range(8):
                ins = nc.vector.tensor_tensor_scan(out=cum[:, t, :], data0=sq_part[:, :], data1=cum[:, t, :],
                                                   initial=0.0, op0=ALU.mult, op1=ALU.add)
            ins.then_inc(ls_vec, 1)
            qk_group(2)
            lo_group(C_QK + 12)
            dve.wait_ge(ls_vec, 3)

            adds = [0]

            def step(ins):
                ins.then_inc(lev_add, 1)
                adds[0] += 1

            def halves(tile, s):
                return tile.rearrange("p k (b h r) -> p (k b) h r", h=2, r=s)

            def level_exponents(n):
                s = LEVELS[n]
                c, d = halves(cum[:, :, :], s), halves(dec[:, :, :], s)
                blocks = 8 * T // (2 * s)
                ref = c[:, :, 0, s - 1:s].broadcast_to([P, blocks, s])
                if n >= 1:
                    dve.wait_ge(lev_mm, n + 1)
                nc.vector.tensor_tensor(d[:, :, 0, :], ref, c[:, :, 0, :], ALU.subtract).then_inc(lev_diff, 1)
                nc.vector.tensor_tensor(d[:, :, 1, :], c[:, :, 1, :], ref, ALU.subtract).then_inc(lev_diff, 1)

            def level_operands(n):
                s = LEVELS[n]
                d, q, k = (halves(z, s) for z in (dec[:, :, :], q_t, k_t))
                dve.wait_ge(lev_exp, n + 1)
                nc.vector.tensor_tensor(d[:, :, 0, :], d[:, :, 0, :], k[:, :, 0, :], ALU.mult).then_inc(lev_mul, 1)
                nc.vector.tensor_tensor(d[:, :, 1, :], d[:, :, 1, :], q[:, :, 1, :], ALU.mult).then_inc(lev_mul, 1)

            def level_add(n):
                s = LEVELS[n]
                dve.wait_ge(lev_mm, n + 2)
                if n == 0:
                    step(nc.vector.tensor_copy(s_off[:, :, :], pair_s[1][:, :].rearrange("p (h i) -> p h i", i=P)))
                    return
                pr = pair_s[(n + 1) % 2][:, :].rearrange("p (h i) -> p h i", i=64)
                mask = masks[:, n - 1:n, :].broadcast_to([P, 8, 64])
                step(nc.vector.tensor_tensor(pr, pr, mask, ALU.mult))
                dve.wait_ge(lev_add, adds[0])
                sd = s_diag[:, :, :].rearrange("p k (b h r) -> p (k b) h r", h=2, r=s)[:, :, 1, :]
                pr2 = pair_s[(n + 1) % 2][:, :].rearrange("p (b r) -> p b r", r=s)
                step(nc.vector.tensor_tensor(sd, sd, pr2, ALU.add))

            level_exponents(0)
            qk_group(3)
            dve.wait_ge(lev_mm, 1)
            dve.wait_ge(consts, 19)
            for a in range(2):
                step(nc.vector.tensor_tensor(s_diag[:, 4 * a:4 * a + 4, :], pair_s[a][:, :].rearrange("p (h i) -> p h i", i=P),
                                             over(ident[:, :], 4),
                                             ALU.mult))
            dve.wait_ge(lev_add, 2)
            for n in range(len(LEVELS)):
                if n >= 1:
                    level_exponents(n)
                    level_add(n - 1)
                level_operands(n)
            level_add(len(LEVELS) - 1)

            def head_sum(h):
                dve.wait_ge(sq_done, 16 + h + 1)
                nc.vector.tensor_reduce(head_sq[h], o_sq[:, h, :, :].rearrange("p k t -> p t k"), AX_X,
                                        ALU.add).then_inc(sum_done, 1)

            for h in range(HEADS):
                dve.wait_ge(pv_done, h + 1)
                nc.vector.tensor_copy(act[:, 4 * h:4 * h + 4, :], slot[h % 2][:, :, :]).then_inc(acc_read[h % 2], 1)
                if h >= 1:
                    head_sum(h - 1)
            head_sum(HEADS - 1)
            lo_group(C_R, wait_order=True)
            for h in range(HEADS):
                invert(4 + h, head_rstd[h])
                for b in range(4):
                    ins = nc.vector.scalar_tensor_tensor(out=act[:, 4 * h + b, :], in0=act[:, 4 * h + b, :],
                                                         scalar=vcol("head_g", 4 * h + b), in1=head_rstd[h],
                                                         op0=ALU.mult, op1=ALU.mult)
                ins.then_inc(o_norm, 1)
            for h in range(HEADS):
                if h >= 1:
                    lo_group(C_R + 4 * h)
                dve.wait_ge(w_used, C_R + 4 * h + 4)
                if h == 0:
                    dve.wait_ge(pv_done, HEADS)
                else:
                    dve.wait_ge(z_done, 4 + h)
                nc.vector.tensor_tensor(tmp[0][:, :, :], slot[h % 2][:, :, :], over(rstd[:, :], 4),
                                        ALU.mult).then_inc(acc_read[h % 2], 1)
                dve.wait_ge(silu_done, HID_GLA + h + 1)
                dve.wait_ge(o_norm, h + 1)
                nc.vector.tensor_tensor(tmp[1][:, :, :], tmp[0][:, :, :], act[:, 4 * h:4 * h + 4, :],
                                        ALU.mult).then_inc(z_done, 1)
                dve.wait_ge(hid_hi, HID_GLA + h + 1)
                nc.vector.tensor_tensor(h_lo[:, 4 * h:4 * h + 4, :], tmp[1][:, :, :],
                                        h_hi[:, 4 * h:4 * h + 4, :].bitcast(F32), ALU.subtract).then_inc(hid_ready, 1)
            residual_and_squares(C_GLA_OUT, U_GLA_OUT, 20, ("norm_ffn", KT, 4 * KT))
            ffn(1, 24, 8, None)
            invert(9, rstd_tok[:, :])
            for g, part in ((0, 1), (1, 2), (2, 3), (3, 4)):
                dve.wait_ge(out_t, part)
                nc.vector.tensor_scalar(out_rows[:, 0, g * GW:(g + 1) * GW], out_bank[g][0], rstd_tok[:, 0:1], None,
                                        ALU.mult).then_inc(rows_out[0], 1)

        @block.tensor
        def _(pe):
            mm = nc.tensor.matmul

            def free_slot(s, use2):
                pe.wait_ge(acc_read[s], use2)

            def chunk(k, s, x1, x2, k0, first, last, ready=None):
                for kt in range(4):
                    if ready is not None:
                        pe.wait_ge(ready[0], ready[1] + kt * ready[2] + 1)
                    for nb in range(4):
                        cols = slice(nb * P, nb * P + P)
                        for i, (w, xx) in enumerate(((w_hi, x1), (w_hi, x2), (w_lo, x1))):
                            ins = mm(slot[s][:, nb, :], w[k][:, kt, cols], xx[:, k0 + kt, :],
                                     start=(first and kt == 0 and i == 0 and nb % 2 == 0),
                                     stop=(last and kt == 3 and i == 2), skip_group_check=True)
                ins.then_inc(w_used, 1)

            def group(c0, k0, s, chunks, x1, x2, ready, per_chunk=False):
                for j in range(chunks):
                    pe.wait_ge(lo_done, c0 + j + 1)
                    if per_chunk:
                        pe.wait_ge(ready[0], ready[1] + j + 1)
                        rd = None
                    else:
                        rd = (ready[0], ready[1] + 4 * j, 1)
                    chunk((k0 + j) % RING, s, x1, x2, 4 * j, j == 0, j == chunks - 1, rd)

            def statistic(to, src, ready, count):
                pe.wait_ge(ready, count)
                mm(to, ones[:, :], src, start=True, stop=True).then_inc(stat_done, 1)

            pe.wait_ge(consts, 5)
            pe.wait_ge(rows_in, 16 * 12)
            nc.tensor.transpose(misc[:, 0:P], vec_rows[:, 0, :], ident[:, :])
            nc.tensor.transpose(misc[:, P:VROWS], vec_rows[0:VROWS - P, 1, :], ident[0:VROWS - P, 0:VROWS - P]).then_inc(par_t, 1)
            for k in range(KT):
                ins = nc.tensor.transpose(pair_s[0][:, k * TAPS:(k + 1) * TAPS], dw_rows[:, k * P:(k + 1) * P],
                                          ident[0:TAPS, 0:TAPS])
            ins.then_inc(par_t, 1)
            for g in range(4):
                if g >= 2:
                    free_slot(g % 2, g // 2)
                for b in range(4):
                    for a in range(2):
                        c = 4 * g + b
                        ins = nc.tensor.transpose(slot[g % 2][:, b, a * P:(a + 1) * P], x_rows[:, a, c * P:(c + 1) * P],
                                                  ident[:, :])
                ins.then_inc(x_t, 1)
            statistic(stat[:, 0, :], sq_sum[:, :], sum_done, 4)

            def conv_taps(tile, t):
                pe.wait_ge(diag_done, tile + 1)
                pe.wait_ge(ulo_done, tile + 1)
                for j in range(PE_TAPS):
                    for n, (w, uu) in enumerate(((diag_hi, u_hi), (diag_hi, u_lo), (diag_lo, u_hi))):
                        ins = mm(pair_s[t][:, 0:T], w[:, t, j, :], uu[:, t, j:j + T],
                                 start=(j == 0 and n == 0), stop=(j == PE_TAPS - 1 and n == 2))
                ins.then_inc(pe_taps, 1)

            def conv_product(i, t):
                free_slot(t, U_CONV_IN // 2 + i)
                for h in range(2):
                    k = 2 * t + h
                    pe.wait_ge(lo_done, 4 * i + k + 1)
                    for kt in range(KT):
                        if isinstance(i, int) and k == 0:
                            pe.wait_ge(x_ready, kt + 1)
                        for j, (w, xx) in enumerate(((w_hi, x_hi), (w_hi, x_lo), (w_lo, x_hi))):
                            ins = mm(slot[t][:, 2 - 2 * h, :], conv_view(w[k])[:, kt, :], xx[:, kt, :],
                                     start=(kt == 0 and j == 0), stop=(kt == KT - 1 and j == 2))
                    ins.then_inc(w_used, 1)

            conv_product(0, 0)
            conv_product(0, 1)
            conv_taps(0, 0)
            with pe.Fori(1, KT // 2) as i:
                conv_product(i, 0)
                conv_taps(2 * i - 1, 1)
                conv_product(i, 1)
                conv_taps(2 * i, 0)
            conv_taps(KT - 1, 1)
            statistic(stat[:, 0, :], y_sum[:, :], ysum_done, KT + 1)
            statistic(stat[:, 1, :], sq_sum[:, :], sum_done, 8)

            def residual_product(c0, u0, x1, x2, ready, per_chunk, chunks=4):
                if chunks == RING:
                    with pe.Fori(0, 2) as i:
                        for s in range(2):
                            free_slot(s, u0 // 2 + i)
                            group(c0 + 4 * s + 8 * i, 0, s, 4, x1, x2, ready, per_chunk)
                else:
                    for g in range(4):
                        free_slot(g % 2, (u0 + g) // 2)
                        group(c0 + chunks * g, c0 + chunks * g, g % 2, chunks, x1, x2, ready, per_chunk)

            def ffn(l, x0, n_sum):
                for pt, (first, pairs) in enumerate(PARTS):
                    c0, u0, h0 = C_FFN[l] + 48 * pt, U_FFN[l] + 12 * pt, HID[l] + first
                    def half(p, s):
                        free_slot(s, u0 // 2 + p)
                        group(c0 + 4 * s + 8 * p, 0, s, 4, x_hi, x_lo, (x_ready, x0))

                    if pt == 0:
                        half(0, 0)
                        statistic(stat[:, 0, :], sq_sum[:, :], sum_done, n_sum)
                        half(0, 1)
                    with pe.Fori(1 if pt == 0 else 0, pairs) as p:
                        for s in range(2):
                            half(p, s)
                    residual_product(c0 + 8 * pairs, u0 + 2 * pairs, h_hi, h_lo, (hid_ready, h0), True, pairs)

            residual_product(C_CONV_OUT, U_CONV_OUT, h_hi, h_lo, (x_ready, KT), False)
            ffn(0, 2 * KT, 12)

            def qk_product(g):
                free_slot(g % 2, (U_QK + g) // 2)
                group(C_QK + 4 * g, 0, g % 2, 4, x_hi, x_lo, (x_ready, 3 * KT))

            qk_product(0)
            statistic(stat[:, 0, :], sq_sum[:, :], sum_done, 16)
            pe.wait_ge(gate_split, 2)
            for k in range(KT):
                for j, (w, xx) in enumerate(((gate_w1_hi, x_hi), (gate_w1_hi, x_lo), (gate_w1_lo, x_hi))):
                    mm(misc[0:RANK, 0:T], w[:, k, :], xx[:, k, :], start=(k == 0 and j == 0), stop=(k == KT - 1 and j == 2))
            pe.wait_ge(rstd_done, 4)
            for a in range(2):
                ins = mm(misc[:, T + a:T + a + 1], rstd[:, a * P:(a + 1) * P], ident[:, 0:1], start=True, stop=True)
            ins.then_inc(z1_done, 1)
            qk_product(1)
            pe.wait_ge(gate_in, 32)
            pe.wait_ge(z1_read, 2)
            for n in range(4):
                for b in range(2):
                    t = 2 * n + b
                    ins = mm(z_bank[n][:, b * T:(b + 1) * T], gate_w2[:, t * P:(t + 1) * P], gate_z1[:, :], start=True, stop=True)
                ins.then_inc(z_ready, 1)
            qk_product(2)
            qk_product(3)

            def self_scores():
                pe.wait_ge(z_read, 4)
                pe.wait_ge(acc_read[1], (U_QK + 3) // 2 + 1)
                for a in range(2):
                    for h in range(HEADS):
                        for kk in range(2):
                            tok = slice(a * P, (a + 1) * P)
                            ins = mm(pair_s[a][:, h * P:(h + 1) * P], k_t[:, 2 * h + kk, tok], q_t[:, 2 * h + kk, tok],
                                     start=(kk == 0), stop=(kk == 1))
                ins.then_inc(lev_mm, 1)

            def level_products(n):
                s = LEVELS[n]
                pe.wait_ge(lev_mul, 2 * (n + 1))
                pe.wait_ge(lev_add, 2 if n <= 1 else 3 + 2 * (n - 2))
                if n == 0:
                    for h in range(HEADS):
                        for kk in range(2):
                            ins = mm(pair_s[1][:, h * P:(h + 1) * P], dec[:, 2 * h + kk, 0:P], dec[:, 2 * h + kk, P:T],
                                     start=(kk == 0), stop=(kk == 1))
                else:
                    pr = pair_s[(n + 1) % 2]
                    for a in range(2):
                        for h in range(HEADS):
                            for kk in range(2):
                                d = dec[:, 2 * h + kk, a * P:(a + 1) * P]
                                ins = mm(pr[:, (4 * a + h) * 64:(4 * a + h + 1) * 64], d,
                                         d.rearrange("p (b h r) -> p b h r", h=2, r=s)[:, :, 1, :],
                                         start=(kk == 0), stop=(kk == 1))
                ins.then_inc(lev_mm, 1)

            for g in range(HEADS):
                free_slot(g % 2, (U_V + g) // 2)
                rows_ = slot[g % 2][:, :, :].rearrange("p (a b) t -> p a (b t)", a=2)
                for j in range(4):
                    pe.wait_ge(lo_done, C_V + 4 * g + j + 1)
                    for kt in range(4):
                        for a in range(2):
                            tok = slice(a * P, (a + 1) * P)
                            for i, (w, xx) in enumerate(((w_hi, x_hi), (w_lo, x_hi), (w_hi, x_lo))):
                                ins = mm(rows_[:, a, :], xx[:, 4 * j + kt, tok], w[j][:, kt, :],
                                         start=(j == 0 and kt == 0 and i == 0), stop=(j == 3 and kt == 3 and i == 2))
                    ins.then_inc(w_used, 1)
                    if g == 0 and j == 0:
                        self_scores()
                    if j % 2 == 1:
                        level_products(2 * g + j // 2)
            pe.wait_ge(lev_add, 3 + 2 * 7)
            for h in range(HEADS):
                free_slot(h % 2, (U_PV + h) // 2)
                if h == 0:
                    pe.wait_ge(acc_read[1], (U_V + 3) // 2 + 1)
                for b in range(4):
                    cols = slice(h * DV + b * P, h * DV + (b + 1) * P)
                    mm(slot[h % 2][:, b, 0:P], v[:, 0, cols], s_diag[:, h, :], start=True, stop=True, skip_group_check=True)
                    mm(slot[h % 2][:, b, P:T], v[:, 0, cols], s_off[:, h, :], start=True, stop=False, skip_group_check=True)
                    ins = mm(slot[h % 2][:, b, P:T], v[:, 1, cols], s_diag[:, 4 + h, :], start=False, stop=True,
                             skip_group_check=True)
                ins.then_inc(pv_done, 1)

            def gate_product(g):
                free_slot(g % 2, (U_R + g) // 2)
                group(C_R + 4 * g, 0, g % 2, 4, x_hi, x_lo, (x_ready, 3 * KT))

            gate_product(0)
            for h in range(HEADS):
                statistic(head_stat[h], head_sq[h], sum_done, 17 + h)
            for g in range(1, HEADS):
                gate_product(g)
            residual_product(C_GLA_OUT, U_GLA_OUT, h_hi, h_lo, (hid_ready, HID_GLA), True)
            ffn(1, 4 * KT, 24)

            def output_rows(g, a):
                for b in range(4):
                    pe.wait_ge(xn_done, 2 * KT + 4 * g + b + 1)
                    ins = nc.tensor.transpose(out_bank[g][a][:, b * P:(b + 1) * P], act[:, 4 * g + b, a * P:(a + 1) * P],
                                              ident[:, :])
                return ins

            free_slot(0, U_OUT // 2)
            output_rows(0, 0)
            output_rows(0, 1).then_inc(out_t, 1)
            output_rows(1, 0)
            output_rows(1, 1).then_inc(out_t, 1)
            output_rows(2, 0).then_inc(out_t, 1)
            pe.wait_ge(sum_done, 28)
            for a in range(2):
                ins = mm(stat[:, 0, a:a + 1], sq_sum[:, a * P:(a + 1) * P], ones[:, 0:1], start=True, stop=True)
            ins.then_inc(stat_done, 1)
            free_slot(1, U_OUT // 2)
            output_rows(3, 0)
            output_rows(3, 1).then_inc(out_t, 1)
            pe.wait_ge(root_done, 10)
            output_rows(2, 1).then_inc(out_t, 1)


_INS = ["x", "norm_mix_g", "norm_ffn_g", "conv_w_in", "conv_b_in", "conv_w_dw", "conv_b_dw", "conv_ln_g", "conv_ln_b",
        "conv_w_out", "conv_b_out", "gla_w_in", "gla_gate_w1", "gla_gate_w2", "gla_gate_b", "gla_head_norm_g",
        "gla_w_out", "ffn_w_gate_up", "ffn_w_down", "final_norm_g"]


def kernel(**inputs):
    import numpy as _np
    import concourse.bacc as _bacc
    from concourse.bass_utils import run_bass_kernel_spmd as _run

    nc = _bacc.Bacc("TRN2", target_bir_lowering=False, num_devices=1)
    arrays, args = {}, []
    for name in _INS:
        a = _np.ascontiguousarray(inputs[name])
        arrays[f"in_{name}"] = a
        args.append(nc.dram_tensor(f"in_{name}", a.shape, mybir.dt.from_np(a.dtype), kind="ExternalInput").ap())
    args.append(nc.dram_tensor("out_0", (1, T, D), F32, kind="ExternalOutput").ap())
    trunk(nc, *args)
    r = _run(nc, [arrays], core_ids=[0])
    return r.results[0]["out_0"]
```

```python
from contextlib import ExitStack

import concourse.bass as bass
from concourse import mybir

F32 = mybir.dt.float32
F32R = mybir.dt.float32r
ALU = mybir.AluOpType
ACT = mybir.ActivationFunctionType
AX_X = mybir.AxisListType.X
ds = bass.ds

P = 128
T = 256
D = 2048
KT = D // P
FF = 5632
TAPS = 31
PAD = TAPS - 1
PE_TAPS = 4
MORE_TAPS = 8
STEPS = TAPS - PE_TAPS + 1
LAST_STEPS = STEPS - MORE_TAPS
UW = T + PE_TAPS + MORE_TAPS
HEADS = 4
DK = 256
DV = 512
RANK = 16
EPS = 1e-6
GATE_DIV = 16.0
RING = 4
AHEAD = RING - 1
GW = 512
PARTS = ((0, 4), (4, 4), (8, 3))

C_CONV_IN = 0
C_CONV_OUT = C_CONV_IN + 32
C_FFN = (C_CONV_OUT + 16, C_CONV_OUT + 16 + 132 + 64)
C_QK = C_FFN[0] + 132
C_V = C_QK + 16
C_R = C_V + 16
C_GLA_OUT = C_R + 16
C_END = C_FFN[1] + 132

U_X = 0
U_CONV_IN = U_X + 4
U_CONV_OUT = U_CONV_IN + 16
U_FFN = (U_CONV_OUT + 4, U_CONV_OUT + 4 + 34 + 20)
U_QK = U_FFN[0] + 34
U_V = U_QK + 4
U_PV = U_V + 4
U_R = U_PV + 4
U_GLA_OUT = U_R + 4
U_OUT = U_FFN[1] + 34

VECTORS = (("norm_mix", 32), ("norm_ffn", 32), ("conv_b_in", 32), ("conv_b_dw", 16), ("ln_g", 16),
           ("conv_b_out", 16), ("ln_b", 16), ("gate_b", 8), ("head_g", 16), ("final_g", 16))
VCOL = {}
_at = 0
for _name, _rows in VECTORS:
    VCOL[_name] = _at
    _at += _rows
VROWS = _at
LEVELS = (128, 64, 32, 16, 8, 4, 2, 1)
HID = (0, 11 + HEADS)
HID_GLA = 11
STAT = (1, 3, 4, 5, 6, 7, 8, 9, 10, 11)


def trunk(nc, x, norm_mix_g, norm_ffn_g, conv_w_in, conv_b_in, conv_w_dw, conv_b_dw, conv_ln_g, conv_ln_b,
          conv_w_out, conv_b_out, gla_w_in, gla_gate_w1, gla_gate_w2, gla_gate_b, gla_head_norm_g,
          gla_w_out, ffn_w_gate_up, ffn_w_down, final_norm_g, out):
    with ExitStack() as ctx:
        base = (nc.sbuf_base + 63) // 64 * 64

        def sb(name, shape, offset, dt=F32):
            return nc.alloc_sbuf_tensor_at(name, shape, dt, offset=base + offset)

        def sem(name):
            return ctx.enter_context(nc.semaphore(name))

        K = 1024
        res = sb("res", [P, KT, T], 0)
        x_hi = sb("x_hi", [P, KT, T], 16 * K, F32R)
        x_lo = sb("x_lo", [P, KT, T], 32 * K, F32R)
        act = sb("act", [P, KT, T], 48 * K)
        h_hi = sb("h_hi", [P, 16, T], 64 * K, F32R)
        h_lo = sb("h_lo", [P, 16, T], 80 * K, F32R)
        raw = [sb(f"raw{i}", [P, 4, GW], (96 + 8 * i) * K) for i in range(RING)]
        w_hi = [sb(f"w_hi{i}", [P, 4, GW], (128 + 8 * i) * K, F32R) for i in range(RING)]
        w_lo = [sb(f"w_lo{i}", [P, 4, GW], (160 + 8 * i) * K, F32R) for i in range(RING)]
        tmp = [sb(f"tmp{i}", [P, 4, T], (192 + 4 * i) * K) for i in range(2)]
        small = 200 * K
        vec = sb("vec", [P, VROWS], small)
        masks = sb("masks", [P, 7, 64], small + 832)
        ones = sb("ones", [P, P], small + 2624)
        ident = sb("ident", [P, P], small + 3136)
        rstd = sb("rstd", [P, T], small + 3648)
        sq_part = sb("sq_part", [P, T], small + 4672)
        sq_sum = sb("sq_sum", [P, T], small + 5696)
        eps = sb("eps", [P, 1], small + 6720)
        rstd_tok = sb("rstd_tok", [P, 2], small + 6752)
        assert base + small + 6784 <= nc.sbuf_usable_end

        x_rows = sb("x_rows", [P, 2, D], 64 * K)
        vec_rows = sb("vec_rows", [P, 2, P], 80 * K)
        dw_rows = sb("dw_rows", [TAPS, D], 81 * K)
        dw = sb("dw", [P, KT * TAPS], 89 * K)
        u = sb("u", [P, 2, PAD + T], 64 * K)
        gate = sb("gate", [P, 2, T], 67 * K)
        y_even = sb("y_even", [P, 2, T], 70 * K)
        y_odd = sb("y_odd", [P, 2, T], 78 * K)
        u_hi = sb("u_hi", [P, 2, UW], 73 * K + 512, F32R)
        u_lo = sb("u_lo", [P, 2, UW], 75 * K + 768, F32R)
        more_hi = sb("more_hi", [P, MORE_TAPS, P], 84 * K, F32R)
        more_lo = sb("more_lo", [P, MORE_TAPS, P], 196 * K, F32R)
        diag_hi = sb("diag_hi", [P, 2, PE_TAPS, P], 80 * K, F32R)
        diag_lo = sb("diag_lo", [P, 2, PE_TAPS, P], 192 * K, F32R)
        dw_hi = sb("dw_hi", [P, KT * TAPS], 91 * K, F32R)
        dw_lo = sb("dw_lo", [P, KT * TAPS], 93 * K)
        y_sum = sb("y_sum", [P, T], 69 * K)
        ln_sq = sb("ln_sq", [P, KT, T], 32 * K)
        v = sb("v", [P, 2, D], 64 * K)
        cum = sb("cum", [P, 8, T], 80 * K)
        dec = sb("dec", [P, 8, T], 88 * K)
        o_sq = sb("o_sq", [P, HEADS, 4, T], 80 * K)
        gate_w1 = sb("gate_w1", [P, KT, RANK], 76 * K)
        gate_w1_hi = sb("gate_w1_hi", [P, KT, RANK], 77 * K, F32R)
        gate_w1_lo = sb("gate_w1_lo", [P, KT, RANK], 78 * K, F32R)
        gate_z1 = sb("gate_z1", [RANK, T], 79 * K)
        gate_w2 = sb("gate_w2", [RANK, HEADS * DK], 92 * K)
        s_diag = sb("s_diag", [P, 2 * HEADS, P], 192 * K)
        s_off = sb("s_off", [P, HEADS, P], 196 * K)
        q_t = act[:, 0:8, :]
        k_t = act[:, 8:16, :]
        out_rows = sb("out_rows", [P, 2, D], 64 * K)

        slot = [ctx.enter_context(nc.psum_tensor(f"slot{i}", [P, 4, T], F32)) for i in range(2)]
        stat = ctx.enter_context(nc.psum_tensor("stat", [P, 2, T], F32))
        pair_s = [ctx.enter_context(nc.psum_tensor(f"pair_s{i}", [P, 512], F32)) for i in range(2)]
        misc = ctx.enter_context(nc.psum_tensor("misc", [P, 512], F32))

        raw_in = [sem(f"raw_in{i}") for i in range(RING)]
        hi_done = sem("hi_done")
        lo_done = sem("lo_done")
        w_used = sem("w_used")
        acc_read = [sem(f"acc_read{i}") for i in range(2)]
        x_in = [sem(f"x_in{g}") for g in range(4)]
        rows_in = sem("rows_in")
        dw_in = sem("dw_in")
        gate_in = sem("gate_in")
        consts = sem("consts")
        gate_split = sem("gate_split")
        par_t = sem("par_t")
        par_read = sem("par_read")
        row_sq = sem("row_sq")
        row_sum = sem("row_sum")
        rstd_diag = sem("rstd_diag")
        x_t = sem("x_t")
        sq_done = sem("sq_done")
        sum_done = sem("sum_done")
        stat_done = sem("stat_done")
        root_done = sem("root_done")
        rstd_done = sem("rstd_done")
        xn_done = sem("xn_done")
        xhi_done = sem("xhi_done")
        x_ready = sem("x_ready")
        sig_done = sem("sig_done")
        tap_done = sem("tap_done")
        uhi_done = sem("uhi_done")
        ulo_done = sem("ulo_done")
        diag_done = sem("diag_done")
        pe_taps = sem("pe_taps")
        dw_split = sem("dw_split")
        ysum_done = sem("ysum_done")
        part_done = sem("part_done")
        last_y = sem("last_y")
        cent_done = sem("cent_done")
        cent_sq = sem("cent_sq")
        half_sq = sem("half_sq")
        z_done = sem("z_done")
        hid_hi = sem("hid_hi")
        hid_ready = sem("hid_ready")
        silu_done = sem("silu_done")
        up_scaled = sem("up_scaled")
        z1_done = sem("z1_done")
        z1_read = sem("z1_read")
        z_ready = sem("z_ready")
        z_read = sem("z_read")
        ls_act = sem("ls_act")
        ls_vec = sem("ls_vec")
        lev_diff = sem("lev_diff")
        lev_exp = sem("lev_exp")
        lev_mul = sem("lev_mul")
        lev_mm = sem("lev_mm")
        lev_add = sem("lev_add")
        pv_done = sem("pv_done")
        o_norm = sem("o_norm")
        out_t = sem("out_t")
        rows_out = [sem(f"rows_out{a}") for a in range(2)]
        stored = sem("stored")

        block = ctx.enter_context(nc.Block())

        conv_in_w = conv_w_in[0].rearrange("(k p) n -> p k n", p=P)
        conv_out_w = conv_w_out[0].rearrange("(k p) n -> p k n", p=P)
        gla_in_w = gla_w_in[0].rearrange("(k p) n -> p k n", p=P)
        gla_out_w = gla_w_out[0].rearrange("(k p) n -> p k n", p=P)
        up_w = [ffn_w_gate_up[i].rearrange("(k p) n -> p k n", p=P) for i in range(2)]
        down_w = [ffn_w_down[i].rearrange("(k p) n -> p k n", p=P) for i in range(2)]

        def conv_view(tile):
            return tile[:, :, :].rearrange("p a (b c) -> p (a b) c", c=P)

        def over(row, n):
            return row.unsqueeze(1).broadcast_to([P, n, row.shape[1]])

        head_sq = [sq_sum[:, :], sq_part[:, :], tmp[1][:, 2, :], tmp[1][:, 3, :]]
        head_rstd = [o_sq[:, h, 0, :] for h in range(HEADS)]
        z_bank = [pair_s[0][:, :], pair_s[1][:, :], misc[:, :], stat[:, :, :].rearrange("p a t -> p (a t)")]
        out_bank = [[slot[0][:, 2 * a:2 * a + 2, :].rearrange("p b t -> p (b t)") for a in range(2)],
                    z_bank[0:2], z_bank[2:4],
                    [slot[1][:, 2 * a:2 * a + 2, :].rearrange("p b t -> p (b t)") for a in range(2)]]
        head_stat = [stat[:, 0, :], misc[:, 0:T], pair_s[0][:, 0:T], pair_s[1][:, 0:T]]

        def vcol(name, i):
            return vec[:, VCOL[name] + i:VCOL[name] + i + 1]

        @block.sync
        def _(sp):
            def rows(dst, src):
                sp.dma_start(dst, src).then_inc(rows_in, 16)

            def load(c, k, dst, src, first=False):
                if not first:
                    sp.wait_ge(lo_done, c - RING + 1)
                sp.dma_start(dst, src).then_inc(raw_in[k], 16)

            def matrix(c0, w, col0, groups, chunks=4, k0=0):
                per = 1 if chunks == RING else groups
                with sp.Fori(0, groups // per) as g:
                    for j in range(per * chunks):
                        load(c0 + per * chunks * g + j, j % RING, raw[j % RING][:, :, :],
                             w[:, k0 + 4 * (j % chunks):k0 + 4 * (j % chunks) + 4,
                               ds(col0 + GW * (g * per + j // chunks), GW)])

            def load_x(g):
                sp.dma_start(x_rows[:, :, g * GW:(g + 1) * GW],
                             x[0, :, g * GW:(g + 1) * GW].rearrange("(a p) d -> p a d", p=P)).then_inc(x_in[g], 16)

            load_x(0)
            load_x(1)
            at = 0
            for name, src in (("norm_mix", norm_mix_g), ("norm_ffn", norm_ffn_g), ("conv_b_in", conv_b_in),
                              ("conv_b_dw", conv_b_dw), ("ln_g", conv_ln_g)):
                n = dict(VECTORS)[name]
                rows(vec_rows[at:at + n, 0, :], src.rearrange("a (r c) -> (a r) c", c=P))
                at += n
            assert at == P
            at = 0
            for name, src in (("conv_b_out", conv_b_out), ("ln_b", conv_ln_b), ("gate_b", gla_gate_b),
                              ("head_g", gla_head_norm_g[0]), ("final_g", final_norm_g.rearrange("(a d) -> a d", a=1))):
                n = dict(VECTORS)[name]
                rows(vec_rows[at:at + n, 1, :], src.rearrange("a (r c) -> (a r) c", c=P))
                at += n
            load_x(2)
            load_x(3)
            sp.dma_start(dw_rows[:, :], conv_w_dw[0]).then_inc(dw_in, 16)

            def conv_turn(i, i0, first):
                for t in range(2):
                    for h in range(2):
                        k = 2 * t + h
                        src = conv_in_w[:, :, ds(2 * P * i + (2 * P * i0 + P * t + D * (1 - h)), P)]
                        load(4 * i + (4 * i0 + k), k, conv_view(raw[k]), src, first)

            conv_turn(0, 0, True)
            with sp.Fori(0, KT // 2 - 1) as i:
                conv_turn(i, 1, False)
            matrix(C_CONV_OUT, conv_out_w, 0, 4)

            def ffn(l):
                for pt, (first, pairs) in enumerate(PARTS):
                    c0 = C_FFN[l] + 48 * pt
                    with sp.Fori(0, pairs) as p:
                        for half in range(2):
                            for j in range(4):
                                load(c0 + 8 * p + 4 * half + j, j, raw[j][:, :, :],
                                     up_w[l][:, 4 * j:4 * j + 4, ds(half * FF + GW * first + GW * p, GW)])
                    matrix(c0 + 8 * pairs, down_w[l], 0, 4, chunks=pairs, k0=4 * first)

            ffn(0)
            matrix(C_QK, gla_in_w, 0, 12)
            matrix(C_GLA_OUT, gla_out_w, 0, 4)
            ffn(1)

            for n in range(2):
                for a in range(2):
                    sp.wait_ge(rows_out[a], 2 * n + 2)
                    cols = slice(2 * n * GW, (2 * n + 2) * GW)
                    sp.dma_start(out[0, a * P:(a + 1) * P, cols], out_rows[:, a, cols]).then_inc(stored, 16)
            sp.wait_ge(stored, 64)

        @block.gpsimd
        def _(pool):
            def lo(c, k, wait_order=False):
                if wait_order:
                    pool.wait_ge(lo_done, c)
                pool.wait_ge(hi_done, c + 1)
                nc.gpsimd.tensor_tensor(w_lo[k][:, :, :], raw[k][:, :, :], w_hi[k][:, :, :].bitcast(F32),
                                        ALU.subtract).then_inc(lo_done, 1)

            nc.gpsimd.memset(ident[:, :], 0.0).then_inc(consts, 1)
            nc.gpsimd.memset(ones[:, :], 1.0).then_inc(consts, 1)
            nc.gpsimd.memset(eps[:, :], EPS).then_inc(consts, 1)
            nc.gpsimd.memset(masks[:, :, :], 1.0).then_inc(consts, 1)
            pool.wait_ge(consts, 4)
            nc.gpsimd.affine_select(out=ident[:, :], in_=ident[:, :], compare_op=ALU.not_equal, fill=1.0,
                                    base=0, pattern=[[-1, P]], channel_multiplier=1).then_inc(consts, 1)
            n = 5
            for m, s in enumerate(LEVELS[1:]):
                v3 = masks[:, m, :].rearrange("p (b r) -> p b r", r=s)
                nc.gpsimd.affine_select(out=v3, in_=v3, compare_op=ALU.is_ge, fill=0.0, base=0,
                                        pattern=[[-2 * s, 64 // s], [0, s]], channel_multiplier=1).then_inc(consts, 1)
                n += 1
                pool.wait_ge(consts, n)
                nc.gpsimd.affine_select(out=v3, in_=v3, compare_op=ALU.is_ge, fill=0.0, base=s - 1,
                                        pattern=[[2 * s, 64 // s], [0, s]], channel_multiplier=-1).then_inc(consts, 1)
                n += 1
            for c in range(AHEAD):
                lo(c, c)
            def sum_y(tile, t, done):
                pool.wait_ge(tap_done, done)
                nc.gpsimd.tensor_tensor(act[:, ds(tile, 1), :].rearrange("p a t -> p (a t)"), y_even[:, t, :],
                                        y_odd[:, t, :], ALU.add)
                for n, part in enumerate((y_even, y_odd)):
                    pool.wait_ge(ysum_done, 2 * tile + (n + 1))
                    nc.gpsimd.tensor_tensor(y_sum[:, :], y_sum[:, :], part[:, t, :], ALU.add).then_inc(ysum_done, 1)

            def split_u(tile, t):
                pool.wait_ge(uhi_done, tile + 1)
                if not isinstance(tile, int):
                    pool.wait_ge(pe_taps, tile - 1)
                nc.gpsimd.tensor_tensor(u_lo[:, t, :], u[:, t, 0:UW], u_hi[:, t, :].bitcast(F32),
                                        ALU.subtract).then_inc(ulo_done, 1)

            for t in range(2):
                for h in range(2):
                    lo(AHEAD + 2 * t + h, (AHEAD + 2 * t + h) % RING)
                split_u(t, t)
            with pool.Fori(0, KT // 2 - 1) as i:
                for t in range(2):
                    j = 2 * t + AHEAD
                    lo(4 * i + (4 + j), j % RING)
                    sum_y(2 * i + t, t, 2 * STEPS * i + (STEPS * (t + 1) + 2))
                    lo(4 * i + (5 + j), (j + 1) % RING)
                    split_u(2 * i + (2 + t), t)
            sum_y(KT - 2, 0, STEPS * (KT - 1) + 2)
            pool.wait_ge(w_used, C_FFN[0] + 96)
            pool.dma_start(gate_w1[:, :, :], gla_gate_w1[0].rearrange("(k p) r -> p k r", p=P)).then_inc(gate_in, 16)
            pool.dma_start(gate_w2[:, :], gla_gate_w2[0]).then_inc(gate_in, 16)
            pool.wait_ge(gate_split, 1)
            nc.gpsimd.tensor_tensor(gate_w1_lo[:, :, :], gate_w1[:, :, :], gate_w1_hi[:, :, :].bitcast(F32),
                                    ALU.subtract).then_inc(gate_split, 1)
            for j in range(16):
                lo(C_V + AHEAD + j, (AHEAD + j) % RING, wait_order=(j == 0))

        @block.scalar
        def _(scalar):
            def hi(c4, k):
                scalar.wait_ge(raw_in[k], 16 * c4 + 16)
                if not (isinstance(c4, int) and c4 == 0):
                    scalar.wait_ge(w_used, 4 * c4 + k - RING + 1)
                nc.scalar.activation(w_hi[k][:, :, :], raw[k][:, :, :], ACT.Copy).then_inc(hi_done, 1)

            def hi_group(c0, chunks=4):
                for c in range(c0 + AHEAD, min(c0 + AHEAD + chunks, C_END)):
                    hi(c // RING, c % RING)

            def hi_group_at(c4):
                for j in range(AHEAD, AHEAD + 4):
                    hi(c4 + j // RING, j % RING)

            def root(n, to, src, scale):
                scalar.wait_ge(stat_done, STAT[n])
                nc.scalar.activation(to, src, ACT.Sqrt, bias=eps[:, 0:1], scale=scale).then_inc(root_done, 1)

            def split_tiles(first, end):
                for t in range(first, end):
                    scalar.wait_ge(xn_done, t + 1)
                    nc.scalar.activation(x_hi[:, t, :], act[:, t, :], ACT.Copy).then_inc(xhi_done, 1)

            def squares(use0, n0, g):
                scalar.wait_ge(acc_read[g % 2], (use0 + g) // 2 + 1)
                if g >= 2:
                    scalar.wait_ge(sum_done, n0 + g - 1)
                nc.scalar.activation(tmp[g % 2][:, :, :], res[:, 4 * g:4 * g + 4, :], ACT.Square).then_inc(sq_done, 1)

            def gains(to, signal, name, v0, g):
                for t in range(4 * g, 4 * g + 4):
                    nc.scalar.activation(to[:, t, :], res[:, t, :], ACT.Copy, scale=vcol(name, v0 + t)).then_inc(signal, 1)

            squared = act[:, :, :].rearrange("p k t -> p (k t)")
            for g in range(4):
                scalar.wait_ge(x_in[g], 16)
                for a in range(2):
                    ins = nc.scalar.activation(squared[:, (2 * g + a) * GW:(2 * g + a + 1) * GW],
                                               x_rows[:, a, g * GW:(g + 1) * GW], ACT.Square,
                                               accum_out=sq_part[:, 4 * a + g:4 * a + g + 1])
                ins.then_inc(row_sq, 1)
            scalar.wait_ge(row_sum, 1)
            nc.scalar.activation(rstd_tok[:, :], sq_part[:, 8:10], ACT.Sqrt, bias=eps[:, 0:1],
                                 scale=1.0 / D).then_inc(root_done, 1)
            scalar.wait_ge(x_t, 4)
            nc.scalar.activation(res[:, 12:16, :], slot[1][:, :, :], ACT.Copy).then_inc(acc_read[1], 1)
            hi(0, 0)
            split_tiles(0, KT // 2)
            hi(0, 1)
            split_tiles(KT // 2, KT)
            hi(0, 2)

            def diagonals(tile, t):
                for j in range(PE_TAPS):
                    for parts, weights in ((diag_hi, dw), (diag_lo, dw_lo)):
                        ins = nc.scalar.activation(parts[:, t, j, :], ident[:, :], ACT.Copy,
                                                   scale=weights[:, ds(TAPS * tile + j, 1)])
                ins.then_inc(diag_done, 1)

            def conv_turn(i):
                for t in range(2):
                    j = 2 * t + AHEAD
                    hi(i + j // RING, j % RING)
                    scalar.wait_ge(w_used, 4 * i + 2 * t + 1)
                    scalar.wait_ge(acc_read[t], U_CONV_IN // 2 + i)
                    nc.scalar.activation(gate[:, t, :], slot[t][:, 2, :], ACT.Sigmoid,
                                         bias=vec[:, ds(VCOL["conv_b_in"] + KT + t + 2 * i, 1)]).then_inc(sig_done, 1)
                    if not (isinstance(i, int) and i == 0):
                        scalar.wait_ge(pe_taps, 2 * i + t - 1)
                    diagonals(2 * i + t, t)
                    hi(i + (j + 1) // RING, (j + 1) % RING)
                    scalar.wait_ge(acc_read[t], U_CONV_IN // 2 + 1 + i)
                    nc.scalar.activation(u_hi[:, t, :], u[:, t, 0:UW], ACT.Copy).then_inc(uhi_done, 1)

            scalar.wait_ge(par_read, 2)
            nc.scalar.activation(dw_hi[:, :], dw[:, :], ACT.Copy).then_inc(dw_split, 1)
            scalar.wait_ge(dw_split, 2)
            conv_turn(0)
            with scalar.Fori(1, KT // 2) as i:
                conv_turn(i)
            for j in range(MORE_TAPS):
                for parts, weights in ((more_hi, dw), (more_lo, dw_lo)):
                    ins = nc.scalar.activation(parts[:, j, :], ident[:, :], ACT.Copy,
                                               scale=weights[:, TAPS * (KT - 1) + PE_TAPS + j:TAPS * (KT - 1) + PE_TAPS + j + 1])
            ins.then_inc(diag_done, 1)
            for g in range(4):
                scalar.wait_ge(cent_done, g + 1)
                nc.scalar.activation(ln_sq[:, 4 * g:4 * g + 4, :], act[:, 4 * g:4 * g + 4, :], ACT.Square).then_inc(cent_sq, 1)
            root(1, rstd[:, :], misc[:, 0:T], 1.0 / D)
            for t in range(KT):
                scalar.wait_ge(z_done, t + 1)
                nc.scalar.activation(act[:, t, :], act[:, t, :], ACT.Silu, bias=vcol("ln_b", t)).then_inc(xn_done, 1)
                scalar.wait_ge(xn_done, KT + t + 1)
                nc.scalar.activation(h_hi[:, t, :], act[:, t, :], ACT.Copy).then_inc(xhi_done, 1)
            for g in range(4):
                hi_group(C_CONV_OUT + 4 * g)
                squares(U_CONV_OUT, 0, g)
                gains(x_hi, xhi_done, "norm_ffn", 0, g)

            def ffn(l, n_sq, n_root, gain):
                for pt, (first, pairs) in enumerate(PARTS):
                    c0, u0 = C_FFN[l] + 48 * pt, U_FFN[l] + 12 * pt
                    def pair(p, with_root=False):
                        hi_group_at(c0 // 4 + 2 * p)
                        if with_root:
                            root(n_root, rstd[:, :], stat[:, 0, :], 1.0 / D)
                        scalar.wait_ge(acc_read[0], u0 // 2 + p + 1)
                        nc.scalar.activation(tmp[0][:, :, :], tmp[0][:, :, :], ACT.Silu).then_inc(silu_done, 1)
                        hi_group_at(c0 // 4 + 1 + 2 * p)
                        scalar.wait_ge(acc_read[1], u0 // 2 + p + 1)
                        nc.scalar.activation(h_hi[:, ds(4 * p, 4), :], tmp[1][:, :, :], ACT.Copy).then_inc(hid_hi, 1)

                    if pt == 0:
                        pair(0, True)
                    with scalar.Fori(1 if pt == 0 else 0, pairs) as p:
                        pair(p)
                    d0, du = c0 + 8 * pairs, u0 + 2 * pairs
                    if pt < 2:
                        with scalar.Fori(0, 4) as g:
                            hi_group_at(d0 // 4 + g)
                    else:
                        for g in range(4):
                            hi_group(d0 + pairs * g, pairs)
                            squares(du, n_sq, g)
                            gain(g)
                            if l == 0 and g == 0:
                                scalar.wait_ge(gate_in, 32)
                                nc.scalar.activation(gate_w1_hi[:, :, :], gate_w1[:, :, :], ACT.Copy).then_inc(gate_split, 1)

            ffn(0, 4, 2, lambda g: gains(x_hi, xhi_done, "norm_mix", KT, g))

            hi_group(C_QK)
            root(3, rstd[:, :], stat[:, 0, :], 1.0 / D)
            hi_group(C_QK + 4)
            hi_group(C_QK + 8, 1)
            scalar.wait_ge(z_read, 4)
            nc.scalar.activation(dec[:, :, :], cum[:, :, :], ACT.Abs).then_inc(ls_act, 1)
            scalar.wait_ge(ls_act, 1)
            nc.scalar.activation(dec[:, :, :], dec[:, :, :], ACT.Exp, scale=-1.0).then_inc(ls_act, 1)
            hi_group(C_QK + 9, 1)
            scalar.wait_ge(ls_act, 2)
            nc.scalar.activation(dec[:, :, :], dec[:, :, :], ACT.Ln, bias=1.0).then_inc(ls_act, 1)
            hi_group(C_QK + 10, 6)

            def level_exp(n):
                scalar.wait_ge(lev_diff, 2 * (n + 1))
                nc.scalar.activation(dec[:, :, :], dec[:, :, :], ACT.Exp, scale=1.0 / GATE_DIV).then_inc(lev_exp, 1)

            for g in range(4):
                for j in range(4):
                    c = C_V + 4 * g + j + AHEAD
                    hi(c // RING, c % RING)
                    if j % 2 == 0:
                        level_exp(2 * g + j // 2)
                scalar.wait_ge(w_used, C_V + 4 * g + 4)
                if g == 0:
                    scalar.wait_ge(z1_read, 2)
                for a in range(2):
                    ins = nc.scalar.activation(v[:, a, g * DV:(g + 1) * DV],
                                               slot[g % 2][:, 2 * a:2 * a + 2, :].rearrange("p b t -> p (b t)"),
                                               ACT.Copy, scale=rstd_tok[:, a:a + 1])
                ins.then_inc(acc_read[g % 2], 1)
            scalar.wait_ge(lev_mm, len(LEVELS) + 1)
            for h in range(HEADS):
                scalar.wait_ge(acc_read[h % 2], (U_PV + h) // 2 + 1)
                nc.scalar.activation(o_sq[:, h, :, :], act[:, 4 * h:4 * h + 4, :], ACT.Square).then_inc(sq_done, 1)
            for h in range(HEADS):
                hi_group(C_R + 4 * h)
                if h == 0:
                    for n in range(HEADS):
                        root(4 + n, head_rstd[n], head_stat[n], 1.0 / DV)
                scalar.wait_ge(acc_read[h % 2], (U_R + h) // 2 + 1)
                nc.scalar.activation(tmp[0][:, :, :], tmp[0][:, :, :], ACT.Silu).then_inc(silu_done, 1)
                scalar.wait_ge(z_done, KT + h + 1)
                nc.scalar.activation(h_hi[:, 4 * h:4 * h + 4, :], tmp[1][:, :, :], ACT.Copy).then_inc(hid_hi, 1)
            for g in range(4):
                hi_group(C_GLA_OUT + 4 * g)
                squares(U_GLA_OUT, 12, g)
                gains(x_hi, xhi_done, "norm_ffn", KT, g)
            ffn(1, 16, 8, lambda g: gains(act, xn_done, "final_g", 0, g))
            root(9, rstd_tok[:, :], stat[:, 0, 0:2], 1.0 / D)
            scalar.wait_ge(rstd_done, 10)
            for g, part in ((0, 1), (1, 2), (3, 4), (2, 5)):
                scalar.wait_ge(out_t, part)
                nc.scalar.activation(out_rows[:, 1, g * GW:(g + 1) * GW], out_bank[g][1], ACT.Copy,
                                     scale=rstd_tok[:, 1:2]).then_inc(rows_out[1], 1)

        @block.vector
        def _(dve):
            def lo(c, k, wait_order=False):
                if wait_order:
                    dve.wait_ge(lo_done, c)
                dve.wait_ge(hi_done, c + 1)
                nc.vector.tensor_tensor(w_lo[k][:, :, :], raw[k][:, :, :], w_hi[k][:, :, :].bitcast(F32),
                                        ALU.subtract).then_inc(lo_done, 1)

            def lo_group(c0, chunks=4, wait_order=False):
                for j in range(chunks):
                    c = c0 + AHEAD + j
                    if c < C_END:
                        lo(c, c % RING, wait_order and j == 0)

            def lo_group_at(c0, g, step):
                for j in range(4):
                    lo(c0 + AHEAD + j + step * g, (AHEAD + j) % RING)

            def sum_squares(n0, g, src):
                dve.wait_ge(sq_done, n0 + g + 1)
                if g == 0:
                    nc.vector.tensor_reduce(sq_sum[:, :], src.rearrange("p k t -> p t k"), AX_X, ALU.add).then_inc(sum_done, 1)
                    return
                dve.wait_ge(sum_done, n0 + g)
                nc.vector.tensor_reduce(sq_part[:, :], src.rearrange("p k t -> p t k"), AX_X, ALU.add).then_inc(part_done, 1)
                parts[0] += 1
                dve.wait_ge(part_done, parts[0])
                nc.vector.tensor_tensor(sq_sum[:, :], sq_sum[:, :], sq_part[:, :], ALU.add).then_inc(sum_done, 1)

            def invert(n, buf):
                dve.wait_ge(root_done, n + 1)
                nc.vector.reciprocal(buf, buf).then_inc(rstd_done, 1)
                dve.wait_ge(rstd_done, n + 1)

            def rms_tiles(name, v0, n):
                def remainder(t):
                    dve.wait_ge(xhi_done, n + t + 1)
                    nc.vector.tensor_tensor(x_lo[:, t, :], act[:, t, :], x_hi[:, t, :].bitcast(F32),
                                            ALU.subtract).then_inc(x_ready, 1)

                for t in range(KT):
                    if t == 12:
                        dve.wait_ge(acc_read[1], 2)
                    nc.vector.scalar_tensor_tensor(out=act[:, t, :], in0=res[:, t, :], scalar=vcol(name, v0 + t),
                                                   in1=rstd[:, :], op0=ALU.mult, op1=ALU.mult).then_inc(xn_done, 1)
                    if t >= 1:
                        remainder(t - 1)
                remainder(KT - 1)

            def gain_remainders(name, v0, n, g):
                for t in range(4 * g, 4 * g + 4):
                    dve.wait_ge(xhi_done, n + t + 1)
                    nc.vector.scalar_tensor_tensor(out=x_lo[:, t, :], in0=res[:, t, :], scalar=vcol(name, v0 + t),
                                                   in1=x_hi[:, t, :].bitcast(F32), op0=ALU.mult,
                                                   op1=ALU.subtract).then_inc(x_ready, 1)

            parts = [0]

            def residual_from_x(g):
                dve.wait_ge(x_t, g + 1)
                nc.vector.tensor_copy(res[:, 4 * g:4 * g + 4, :], slot[g % 2][:, :, :]).then_inc(acc_read[g % 2], 1)

            residual_from_x(0)
            residual_from_x(1)
            dve.wait_ge(par_t, 1)
            nc.vector.tensor_copy(vec[:, :], misc[:, 0:VROWS]).then_inc(par_read, 1)
            dve.wait_ge(row_sq, 4)
            nc.vector.tensor_reduce(sq_part[:, 8:10], sq_part[:, 0:8].rearrange("p (a g) -> p a g", a=2), AX_X,
                                    ALU.add).then_inc(row_sum, 1)
            invert(0, rstd_tok[:, :])
            for a in range(2):
                ins = nc.vector.tensor_scalar(sq_sum[:, a * P:(a + 1) * P], ident[:, :], rstd_tok[:, a:a + 1], None, ALU.mult)
            ins.then_inc(rstd_diag, 1)
            residual_from_x(2)
            dve.wait_ge(stat_done, 1)
            nc.vector.tensor_copy(rstd[:, :], stat[:, 0, :]).then_inc(rstd_diag, 1)
            dve.wait_ge(rstd_diag, 2)
            rms_tiles("norm_mix", 0, 0)
            dve.wait_ge(par_t, 2)
            nc.vector.tensor_copy(dw[:, :], pair_s[0][:, 0:KT * TAPS]).then_inc(par_read, 1)

            dve.wait_ge(x_t, 4)
            nc.vector.memset(y_sum[:, :], 0.0).then_inc(ysum_done, 1)
            nc.vector.memset(u[:, 0, 0:PAD], 0.0).then_inc(tap_done, 1)
            nc.vector.memset(u[:, 1, 0:PAD], 0.0).then_inc(tap_done, 1)
            def conv_tile(i, t, more=0):
                done = STEPS * t + 2 + 2 * STEPS * i
                dve.wait_ge(sig_done, 2 * i + t + 1)
                dve.wait_ge(w_used, 4 * i + 2 * t + 2)
                dve.wait_ge(tap_done, done)
                if not (isinstance(i, int) and i == 0):
                    dve.wait_ge(ulo_done, 2 * i + t - 1)
                    dve.wait_ge(ysum_done, 4 * i + 2 * t - 1)
                nc.vector.scalar_tensor_tensor(out=u[:, t, PAD:PAD + T], in0=slot[t][:, 0, :],
                                               scalar=vec[:, ds(VCOL["conv_b_in"] + t + 2 * i, 1)],
                                               in1=gate[:, t, :], op0=ALU.add, op1=ALU.mult).then_inc(acc_read[t], 1)
                dve.wait_ge(acc_read[t], U_CONV_IN // 2 + i + 1)
                for n, j in enumerate(range(PE_TAPS + more, TAPS)):
                    acc = (y_even, y_odd)[n % 2][:, t, :]
                    w = dw[:, ds(TAPS * (2 * i + t) + j, 1)]
                    if n == 0:
                        nc.vector.tensor_scalar(acc, u[:, t, j:j + T], w, vec[:, ds(VCOL["conv_b_dw"] + t + 2 * i, 1)],
                                                ALU.mult, ALU.add).then_inc(tap_done, 1)
                    elif n == 1:
                        nc.vector.tensor_scalar(acc, u[:, t, j:j + T], w, None, ALU.mult).then_inc(tap_done, 1)
                    else:
                        dve.wait_ge(tap_done, done + n - 1)
                        nc.vector.scalar_tensor_tensor(out=acc, in0=u[:, t, j:j + T], scalar=w, in1=acc,
                                                       op0=ALU.mult, op1=ALU.add).then_inc(tap_done, 1)
                dve.wait_ge(pe_taps, 2 * i + t + 1)
                early = (y_even, y_odd)[(STEPS - more - 1) % 2][:, t, :]
                dve.wait_ge(tap_done, done + STEPS - more - 2)
                nc.vector.tensor_tensor(early, pair_s[t][:, 0:T], early, ALU.add).then_inc(tap_done, 1)

            dve.wait_ge(dw_split, 1)
            nc.vector.tensor_tensor(dw_lo[:, :], dw[:, :], dw_hi[:, :].bitcast(F32), ALU.subtract).then_inc(dw_split, 1)
            for t in range(2):
                conv_tile(0, t)
            with dve.Fori(1, KT // 2 - 1) as i:
                for t in range(2):
                    conv_tile(i, t)
            conv_tile(KT // 2 - 1, 0)
            conv_tile(KT // 2 - 1, 1, MORE_TAPS)
            dve.wait_ge(tap_done, STEPS * (KT - 1) + LAST_STEPS + 2)
            nc.vector.tensor_tensor(act[:, KT - 1, :], y_even[:, 1, :], y_odd[:, 1, :], ALU.add).then_inc(last_y, 1)

            dve.wait_ge(stat_done, STAT[1] - 1)
            dve.wait_ge(last_y, 1)
            for g in range(4):
                nc.vector.scalar_tensor_tensor(out=act[:, 4 * g:4 * g + 4, :], in0=over(stat[:, 0, :], 4), scalar=-1.0 / D,
                                               in1=act[:, 4 * g:4 * g + 4, :], op0=ALU.mult,
                                               op1=ALU.add).then_inc(cent_done, 1)
            for n, part in enumerate((sq_part, sq_sum)):
                dve.wait_ge(cent_sq, 3 + n)
                nc.vector.tensor_reduce(part[:, :], ln_sq[:, 8 + 4 * n:12 + 4 * n, :].rearrange("p k t -> p t k"), AX_X,
                                        ALU.add).then_inc(half_sq, 1)
            invert(1, rstd[:, :])

            def ln_remainder(t):
                dve.wait_ge(xhi_done, KT + t + 1)
                nc.vector.tensor_tensor(h_lo[:, t, :], act[:, t, :], h_hi[:, t, :].bitcast(F32),
                                        ALU.subtract).then_inc(x_ready, 1)
            for t in range(KT):
                nc.vector.scalar_tensor_tensor(out=act[:, t, :], in0=act[:, t, :], scalar=vcol("ln_g", t), in1=rstd[:, :],
                                               op0=ALU.mult, op1=ALU.mult).then_inc(z_done, 1)
                if t >= 2:
                    ln_remainder(t - 2)
            for t in (KT - 2, KT - 1):
                ln_remainder(t)

            def residual_group(c_end, use, g, bias=None):
                dve.wait_ge(w_used, c_end + 1)
                if bias is None:
                    nc.vector.tensor_tensor(res[:, ds(4 * g, 4), :], slot[use % 2][:, :, :], res[:, ds(4 * g, 4), :],
                                            ALU.add).then_inc(acc_read[use % 2], 1)
                    return
                for b in range(4):
                    ins = nc.vector.scalar_tensor_tensor(out=res[:, 4 * g + b, :], in0=slot[use % 2][:, b, :],
                                                         scalar=vcol(bias, 4 * g + b), in1=res[:, 4 * g + b, :],
                                                         op0=ALU.add, op1=ALU.add)
                ins.then_inc(acc_read[use % 2], 1)

            def residual_and_squares(c0, use0, n0, gains, chunks=4, bias=None, order=False):
                for g in range(4):
                    lo_group(c0 + chunks * g, chunks, wait_order=order and g == 0)
                    residual_group(c0 + chunks * (g + 1) - 1, use0 + g, g, bias)
                    if g >= 1:
                        sum_squares(n0, g - 1, tmp[(g - 1) % 2][:, :, :])
                        if gains:
                            gain_remainders(*gains, g - 1)
                sum_squares(n0, 3, tmp[1][:, :, :])
                if gains:
                    gain_remainders(*gains, 3)

            residual_and_squares(C_CONV_OUT, U_CONV_OUT, 0, ("norm_ffn", 0, 2 * KT), bias="conv_b_out", order=True)

            def ffn(l, n_sq, n_root, gains):
                for pt, (first, pairs) in enumerate(PARTS):
                    c0, u0, h0 = C_FFN[l] + 48 * pt, U_FFN[l] + 12 * pt, HID[l] + first
                    def pair(p, with_root=False):
                        lo_group_at(c0, p, 8)
                        if with_root:
                            invert(n_root, rstd[:, :])
                        dve.wait_ge(w_used, c0 + 8 * p + 4)
                        dve.wait_ge(acc_read[1], u0 // 2 + p)
                        nc.vector.tensor_tensor(tmp[0][:, :, :], slot[0][:, :, :], over(rstd[:, :], 4),
                                                ALU.mult).then_inc(acc_read[0], 1)
                        lo_group_at(c0 + 4, p, 8)
                        dve.wait_ge(silu_done, h0 + p + 1)
                        nc.vector.tensor_tensor(tmp[0][:, :, :], tmp[0][:, :, :], over(rstd[:, :], 4),
                                                ALU.mult).then_inc(up_scaled, 1)
                        dve.wait_ge(up_scaled, 11 * l + first + p + 1)
                        dve.wait_ge(w_used, c0 + 8 * p + 8)
                        nc.vector.tensor_tensor(tmp[1][:, :, :], slot[1][:, :, :], tmp[0][:, :, :],
                                                ALU.mult).then_inc(acc_read[1], 1)
                        dve.wait_ge(hid_hi, h0 + p + 1)
                        nc.vector.tensor_tensor(h_lo[:, ds(4 * p, 4), :], tmp[1][:, :, :],
                                                h_hi[:, ds(4 * p, 4), :].bitcast(F32), ALU.subtract).then_inc(hid_ready, 1)

                    if pt == 0:
                        pair(0, True)
                    with dve.Fori(1 if pt == 0 else 0, pairs) as p:
                        pair(p)
                    d0, du = c0 + 8 * pairs, u0 + 2 * pairs
                    if pt < 2:
                        with dve.Fori(0, 2) as i:
                            for g in range(2):
                                lo_group_at(d0 + 4 * g, i, 8)
                                residual_group(d0 + 4 * g + 3 + 8 * i, g, 2 * i + g)
                    else:
                        residual_and_squares(d0, du, n_sq, gains, chunks=pairs)

            ffn(0, 4, 2, ("norm_mix", KT, 3 * KT))

            def qk_group(g):
                dve.wait_ge(w_used, C_QK + 4 * g + 4)
                nc.vector.scalar_tensor_tensor(out=act[:, 4 * g:4 * g + 4, :], in0=slot[g % 2][:, :, :],
                                               scalar=DK ** -0.5 if g < 2 else 1.0, in1=over(rstd[:, :], 4),
                                               op0=ALU.mult, op1=ALU.mult).then_inc(acc_read[g % 2], 1)

            lo_group(C_QK)
            invert(3, rstd[:, :])
            qk_group(0)
            dve.wait_ge(z1_done, 1)
            nc.vector.tensor_tensor(gate_z1[:, :], misc[0:RANK, 0:T], rstd[0:RANK, :], ALU.mult).then_inc(z1_read, 1)
            nc.vector.tensor_copy(rstd_tok[:, :], misc[:, T:T + 2]).then_inc(z1_read, 1)
            lo_group(C_QK + 4)
            qk_group(1)
            for n in range(4):
                dve.wait_ge(z_ready, n + 1)
                for b in range(2):
                    ins = nc.vector.tensor_scalar(cum[:, 2 * n + b, :], z_bank[n][:, b * T:(b + 1) * T],
                                                  vcol("gate_b", 2 * n + b), None, ALU.add)
                ins.then_inc(z_read, 1)
            lo_group(C_QK + 8)
            nc.vector.memset(sq_part[:, :], 1.0).then_inc(ls_vec, 1)
            dve.wait_ge(ls_act, 3)
            nc.vector.scalar_tensor_tensor(out=cum[:, :, :], in0=cum[:, :, :], scalar=0.0, in1=dec[:, :, :],
                                           op0=ALU.min, op1=ALU.subtract).then_inc(ls_vec, 1)
            dve.wait_ge(ls_vec, 2)
            for t in range(8):
                ins = nc.vector.tensor_tensor_scan(out=cum[:, t, :], data0=sq_part[:, :], data1=cum[:, t, :],
                                                   initial=0.0, op0=ALU.mult, op1=ALU.add)
            ins.then_inc(ls_vec, 1)
            qk_group(2)
            lo_group(C_QK + 12)
            dve.wait_ge(ls_vec, 3)

            adds = [0]

            def step(ins):
                ins.then_inc(lev_add, 1)
                adds[0] += 1

            def halves(tile, s):
                return tile.rearrange("p k (b h r) -> p (k b) h r", h=2, r=s)

            def level_exponents(n):
                s = LEVELS[n]
                c, d = halves(cum[:, :, :], s), halves(dec[:, :, :], s)
                blocks = 8 * T // (2 * s)
                ref = c[:, :, 0, s - 1:s].broadcast_to([P, blocks, s])
                if n >= 1:
                    dve.wait_ge(lev_mm, n + 1)
                nc.vector.tensor_tensor(d[:, :, 0, :], ref, c[:, :, 0, :], ALU.subtract).then_inc(lev_diff, 1)
                nc.vector.tensor_tensor(d[:, :, 1, :], c[:, :, 1, :], ref, ALU.subtract).then_inc(lev_diff, 1)

            def level_operands(n):
                s = LEVELS[n]
                d, q, k = (halves(z, s) for z in (dec[:, :, :], q_t, k_t))
                dve.wait_ge(lev_exp, n + 1)
                nc.vector.tensor_tensor(d[:, :, 0, :], d[:, :, 0, :], k[:, :, 0, :], ALU.mult).then_inc(lev_mul, 1)
                nc.vector.tensor_tensor(d[:, :, 1, :], d[:, :, 1, :], q[:, :, 1, :], ALU.mult).then_inc(lev_mul, 1)

            def level_add(n):
                s = LEVELS[n]
                dve.wait_ge(lev_mm, n + 2)
                if n == 0:
                    step(nc.vector.tensor_copy(s_off[:, :, :], pair_s[1][:, :].rearrange("p (h i) -> p h i", i=P)))
                    return
                pr = pair_s[(n + 1) % 2][:, :].rearrange("p (h i) -> p h i", i=64)
                mask = masks[:, n - 1:n, :].broadcast_to([P, 8, 64])
                step(nc.vector.tensor_tensor(pr, pr, mask, ALU.mult))
                dve.wait_ge(lev_add, adds[0])
                sd = s_diag[:, :, :].rearrange("p k (b h r) -> p (k b) h r", h=2, r=s)[:, :, 1, :]
                pr2 = pair_s[(n + 1) % 2][:, :].rearrange("p (b r) -> p b r", r=s)
                step(nc.vector.tensor_tensor(sd, sd, pr2, ALU.add))

            level_exponents(0)
            qk_group(3)
            dve.wait_ge(lev_mm, 1)
            dve.wait_ge(consts, 19)
            for a in range(2):
                step(nc.vector.tensor_tensor(s_diag[:, 4 * a:4 * a + 4, :], pair_s[a][:, :].rearrange("p (h i) -> p h i", i=P),
                                             over(ident[:, :], 4),
                                             ALU.mult))
            dve.wait_ge(lev_add, 2)
            for n in range(len(LEVELS)):
                if n >= 1:
                    level_exponents(n)
                    level_add(n - 1)
                level_operands(n)
            level_add(len(LEVELS) - 1)

            def head_sum(h):
                dve.wait_ge(sq_done, 8 + h + 1)
                nc.vector.tensor_reduce(head_sq[h], o_sq[:, h, :, :].rearrange("p k t -> p t k"), AX_X,
                                        ALU.add).then_inc(sum_done, 1)

            for h in range(HEADS):
                dve.wait_ge(pv_done, h + 1)
                nc.vector.tensor_copy(act[:, 4 * h:4 * h + 4, :], slot[h % 2][:, :, :]).then_inc(acc_read[h % 2], 1)
                if h >= 1:
                    head_sum(h - 1)
            head_sum(HEADS - 1)
            for h in range(HEADS):
                lo_group(C_R + 4 * h, wait_order=(h == 0))
                dve.wait_ge(w_used, C_R + 4 * h + 4)
                if h == 0:
                    dve.wait_ge(pv_done, HEADS)
                else:
                    dve.wait_ge(z_done, KT + h)
                nc.vector.tensor_tensor(tmp[0][:, :, :], slot[h % 2][:, :, :], over(rstd[:, :], 4),
                                        ALU.mult).then_inc(acc_read[h % 2], 1)
                invert(4 + h, head_rstd[h])
                for b in range(4):
                    ins = nc.vector.scalar_tensor_tensor(out=act[:, 4 * h + b, :], in0=act[:, 4 * h + b, :],
                                                         scalar=vcol("head_g", 4 * h + b), in1=head_rstd[h],
                                                         op0=ALU.mult, op1=ALU.mult)
                ins.then_inc(o_norm, 1)
                dve.wait_ge(silu_done, HID_GLA + h + 1)
                dve.wait_ge(o_norm, h + 1)
                nc.vector.tensor_tensor(tmp[1][:, :, :], tmp[0][:, :, :], act[:, 4 * h:4 * h + 4, :],
                                        ALU.mult).then_inc(z_done, 1)
                dve.wait_ge(hid_hi, HID_GLA + h + 1)
                nc.vector.tensor_tensor(h_lo[:, 4 * h:4 * h + 4, :], tmp[1][:, :, :],
                                        h_hi[:, 4 * h:4 * h + 4, :].bitcast(F32), ALU.subtract).then_inc(hid_ready, 1)
            residual_and_squares(C_GLA_OUT, U_GLA_OUT, 12, ("norm_ffn", KT, 4 * KT))
            ffn(1, 16, 8, None)
            invert(9, rstd_tok[:, :])
            for g, part in ((0, 1), (1, 2), (2, 3), (3, 4)):
                dve.wait_ge(out_t, part)
                nc.vector.tensor_scalar(out_rows[:, 0, g * GW:(g + 1) * GW], out_bank[g][0], rstd_tok[:, 0:1], None,
                                        ALU.mult).then_inc(rows_out[0], 1)

        @block.tensor
        def _(pe):
            mm = nc.tensor.matmul

            def free_slot(s, use2):
                pe.wait_ge(acc_read[s], use2)

            def chunk(k, s, x1, x2, k0, first, last, ready=None):
                for kt in range(4):
                    if ready is not None:
                        pe.wait_ge(ready[0], ready[1] + kt * ready[2] + 1)
                    for nb in range(4):
                        cols = slice(nb * P, nb * P + P)
                        for i, (w, xx) in enumerate(((w_hi, x1), (w_hi, x2), (w_lo, x1))):
                            ins = mm(slot[s][:, nb, :], w[k][:, kt, cols], xx[:, k0 + kt, :],
                                     start=(first and kt == 0 and i == 0 and nb % 2 == 0),
                                     stop=(last and kt == 3 and i == 2), skip_group_check=True)
                ins.then_inc(w_used, 1)

            def group(c0, k0, s, chunks, x1, x2, ready, per_chunk=False):
                for j in range(chunks):
                    pe.wait_ge(lo_done, c0 + j + 1)
                    if per_chunk:
                        pe.wait_ge(ready[0], ready[1] + j + 1)
                        rd = None
                    else:
                        rd = (ready[0], ready[1] + 4 * j, 1)
                    chunk((k0 + j) % RING, s, x1, x2, 4 * j, j == 0, j == chunks - 1, rd)

            def statistic(to, src, ready, count):
                pe.wait_ge(ready, count)
                mm(to, ones[:, :], src, start=True, stop=True).then_inc(stat_done, 1)

            pe.wait_ge(consts, 5)
            def transposed_x(g):
                pe.wait_ge(x_in[g], 16)
                if g >= 2:
                    free_slot(g % 2, g // 2)
                for b in range(4):
                    for a in range(2):
                        c = 4 * g + b
                        ins = nc.tensor.transpose(slot[g % 2][:, b, a * P:(a + 1) * P], x_rows[:, a, c * P:(c + 1) * P],
                                                  ident[:, :])
                ins.then_inc(x_t, 1)

            transposed_x(0)
            transposed_x(1)
            pe.wait_ge(rows_in, 16 * len(VECTORS))
            nc.tensor.transpose(misc[:, 0:P], vec_rows[:, 0, :], ident[:, :])
            nc.tensor.transpose(misc[:, P:VROWS], vec_rows[0:VROWS - P, 1, :], ident[0:VROWS - P, 0:VROWS - P]).then_inc(par_t, 1)
            transposed_x(2)
            transposed_x(3)
            pe.wait_ge(rstd_diag, 1)
            mm(stat[:, 0, :], ones[:, :], sq_sum[:, :], start=True, stop=True).then_inc(stat_done, 1)
            pe.wait_ge(dw_in, 16)
            for k in range(KT):
                ins = nc.tensor.transpose(pair_s[0][:, k * TAPS:(k + 1) * TAPS], dw_rows[:, k * P:(k + 1) * P],
                                          ident[0:TAPS, 0:TAPS])
            ins.then_inc(par_t, 1)

            def conv_taps(tile, t, more=0):
                pe.wait_ge(diag_done, tile + 1)
                pe.wait_ge(ulo_done, tile + 1)
                for j in range(PE_TAPS + more):
                    if j < PE_TAPS:
                        w_h, w_l = diag_hi[:, t, j, :], diag_lo[:, t, j, :]
                    else:
                        w_h, w_l = more_hi[:, j - PE_TAPS, :], more_lo[:, j - PE_TAPS, :]
                    if j == PE_TAPS:
                        pe.wait_ge(diag_done, tile + 2)
                    for n, (w, uu) in enumerate(((w_h, u_hi), (w_h, u_lo), (w_l, u_hi))):
                        ins = mm(pair_s[t][:, 0:T], w, uu[:, t, j:j + T],
                                 start=(j == 0 and n == 0), stop=(j == PE_TAPS + more - 1 and n == 2))
                ins.then_inc(pe_taps, 1)

            def conv_product(i, t):
                free_slot(t, U_CONV_IN // 2 + i)
                for h in range(2):
                    k = 2 * t + h
                    if isinstance(i, int) and k == 0:
                        pe.wait_ge(hi_done, 1)
                        for kt in range(KT):
                            pe.wait_ge(x_ready, kt + 1)
                            for j, xx in enumerate((x_hi, x_lo)):
                                mm(slot[t][:, 2, :], conv_view(w_hi[k])[:, kt, :], xx[:, kt, :],
                                   start=(kt == 0 and j == 0), stop=False)
                        pe.wait_ge(lo_done, 1)
                        for kt in range(KT):
                            ins = mm(slot[t][:, 2, :], conv_view(w_lo[k])[:, kt, :], x_hi[:, kt, :],
                                     start=False, stop=(kt == KT - 1))
                        ins.then_inc(w_used, 1)
                        continue
                    pe.wait_ge(lo_done, 4 * i + k + 1)
                    for kt in range(KT):
                        for j, (w, xx) in enumerate(((w_hi, x_hi), (w_hi, x_lo), (w_lo, x_hi))):
                            ins = mm(slot[t][:, 2 - 2 * h, :], conv_view(w[k])[:, kt, :], xx[:, kt, :],
                                     start=(kt == 0 and j == 0), stop=(kt == KT - 1 and j == 2))
                    ins.then_inc(w_used, 1)

            conv_product(0, 0)
            conv_product(0, 1)
            conv_taps(0, 0)
            with pe.Fori(1, KT // 2) as i:
                conv_product(i, 0)
                conv_taps(2 * i - 1, 1)
                conv_product(i, 1)
                conv_taps(2 * i, 0)
            conv_taps(KT - 1, 1, MORE_TAPS)
            pe.wait_ge(ysum_done, 2 * (KT - 1) + 1)
            mm(stat[:, 0, :], ones[:, :], y_sum[:, :], start=True, stop=False)
            for n, part in enumerate((y_odd, y_even) if LAST_STEPS % 2 else (y_even, y_odd)):
                pe.wait_ge(tap_done, STEPS * (KT - 1) + LAST_STEPS + 1 + n)
                ins = mm(stat[:, 0, :], ones[:, :], part[:, 1, :], start=False, stop=(n == 1))
            ins.then_inc(stat_done, 1)
            for t in range(KT // 2):
                if t % 4 == 0:
                    pe.wait_ge(cent_sq, t // 4 + 1)
                mm(misc[:, 0:T], ones[:, :], ln_sq[:, t, :], start=(t == 0), stop=False)
            for n, part in enumerate((sq_part, sq_sum)):
                pe.wait_ge(half_sq, n + 1)
                ins = mm(misc[:, 0:T], ones[:, :], part[:, :], start=False, stop=(n == 1))
            ins.then_inc(stat_done, 1)

            def residual_product(c0, u0, x1, x2, ready, per_chunk, chunks=4):
                if chunks == RING:
                    with pe.Fori(0, 2) as i:
                        for s in range(2):
                            free_slot(s, u0 // 2 + i)
                            group(c0 + 4 * s + 8 * i, 0, s, 4, x1, x2, ready, per_chunk)
                else:
                    for g in range(4):
                        free_slot(g % 2, (u0 + g) // 2)
                        group(c0 + chunks * g, c0 + chunks * g, g % 2, chunks, x1, x2, ready, per_chunk)

            def ffn(l, x0, n_sum):
                for pt, (first, pairs) in enumerate(PARTS):
                    c0, u0, h0 = C_FFN[l] + 48 * pt, U_FFN[l] + 12 * pt, HID[l] + first
                    def half(p, s):
                        free_slot(s, u0 // 2 + p)
                        group(c0 + 4 * s + 8 * p, 0, s, 4, x_hi, x_lo, (x_ready, x0))

                    if pt == 0:
                        half(0, 0)
                        statistic(stat[:, 0, :], sq_sum[:, :], sum_done, n_sum)
                        half(0, 1)
                    with pe.Fori(1 if pt == 0 else 0, pairs) as p:
                        for s in range(2):
                            half(p, s)
                    residual_product(c0 + 8 * pairs, u0 + 2 * pairs, h_hi, h_lo, (hid_ready, h0), True, pairs)

            residual_product(C_CONV_OUT, U_CONV_OUT, h_hi, h_lo, (x_ready, KT), False)
            ffn(0, 2 * KT, 4)

            def qk_product(g):
                free_slot(g % 2, (U_QK + g) // 2)
                group(C_QK + 4 * g, 0, g % 2, 4, x_hi, x_lo, (x_ready, 3 * KT))

            qk_product(0)
            statistic(stat[:, 0, :], sq_sum[:, :], sum_done, 8)
            pe.wait_ge(gate_split, 2)
            for k in range(KT):
                for j, (w, xx) in enumerate(((gate_w1_hi, x_hi), (gate_w1_hi, x_lo), (gate_w1_lo, x_hi))):
                    mm(misc[0:RANK, 0:T], w[:, k, :], xx[:, k, :], start=(k == 0 and j == 0), stop=(k == KT - 1 and j == 2))
            pe.wait_ge(rstd_done, 4)
            for a in range(2):
                ins = mm(misc[:, T + a:T + a + 1], rstd[:, a * P:(a + 1) * P], ident[:, 0:1], start=True, stop=True)
            ins.then_inc(z1_done, 1)
            qk_product(1)
            pe.wait_ge(gate_in, 32)
            pe.wait_ge(z1_read, 2)
            for n in range(4):
                for b in range(2):
                    t = 2 * n + b
                    ins = mm(z_bank[n][:, b * T:(b + 1) * T], gate_w2[:, t * P:(t + 1) * P], gate_z1[:, :], start=True, stop=True)
                ins.then_inc(z_ready, 1)
            qk_product(2)
            qk_product(3)

            def self_scores():
                pe.wait_ge(z_read, 4)
                pe.wait_ge(acc_read[1], (U_QK + 3) // 2 + 1)
                for a in range(2):
                    for h in range(HEADS):
                        for kk in range(2):
                            tok = slice(a * P, (a + 1) * P)
                            ins = mm(pair_s[a][:, h * P:(h + 1) * P], k_t[:, 2 * h + kk, tok], q_t[:, 2 * h + kk, tok],
                                     start=(kk == 0), stop=(kk == 1))
                ins.then_inc(lev_mm, 1)

            def level_products(n):
                s = LEVELS[n]
                pe.wait_ge(lev_mul, 2 * (n + 1))
                pe.wait_ge(lev_add, 2 if n <= 1 else 3 + 2 * (n - 2))
                if n == 0:
                    for h in range(HEADS):
                        for kk in range(2):
                            ins = mm(pair_s[1][:, h * P:(h + 1) * P], dec[:, 2 * h + kk, 0:P], dec[:, 2 * h + kk, P:T],
                                     start=(kk == 0), stop=(kk == 1))
                else:
                    pr = pair_s[(n + 1) % 2]
                    for a in range(2):
                        for h in range(HEADS):
                            for kk in range(2):
                                d = dec[:, 2 * h + kk, a * P:(a + 1) * P]
                                ins = mm(pr[:, (4 * a + h) * 64:(4 * a + h + 1) * 64], d,
                                         d.rearrange("p (b h r) -> p b h r", h=2, r=s)[:, :, 1, :],
                                         start=(kk == 0), stop=(kk == 1))
                ins.then_inc(lev_mm, 1)

            for g in range(HEADS):
                free_slot(g % 2, (U_V + g) // 2)
                rows_ = slot[g % 2][:, :, :].rearrange("p (a b) t -> p a (b t)", a=2)
                for j in range(4):
                    pe.wait_ge(lo_done, C_V + 4 * g + j + 1)
                    for kt in range(4):
                        for a in range(2):
                            tok = slice(a * P, (a + 1) * P)
                            for i, (w, xx) in enumerate(((w_hi, x_hi), (w_lo, x_hi), (w_hi, x_lo))):
                                ins = mm(rows_[:, a, :], xx[:, 4 * j + kt, tok], w[j][:, kt, :],
                                         start=(j == 0 and kt == 0 and i == 0), stop=(j == 3 and kt == 3 and i == 2))
                    ins.then_inc(w_used, 1)
                    if g == 0 and j == 0:
                        self_scores()
                    if j % 2 == 1:
                        level_products(2 * g + j // 2)
            pe.wait_ge(lev_add, 3 + 2 * 7)
            for h in range(HEADS):
                free_slot(h % 2, (U_PV + h) // 2)
                if h == 0:
                    pe.wait_ge(acc_read[1], (U_V + 3) // 2 + 1)
                for b in range(4):
                    cols = slice(h * DV + b * P, h * DV + (b + 1) * P)
                    mm(slot[h % 2][:, b, 0:P], v[:, 0, cols], s_diag[:, h, :], start=True, stop=True, skip_group_check=True)
                    mm(slot[h % 2][:, b, P:T], v[:, 0, cols], s_off[:, h, :], start=True, stop=False, skip_group_check=True)
                    ins = mm(slot[h % 2][:, b, P:T], v[:, 1, cols], s_diag[:, 4 + h, :], start=False, stop=True,
                             skip_group_check=True)
                ins.then_inc(pv_done, 1)

            def gate_product(g):
                free_slot(g % 2, (U_R + g) // 2)
                group(C_R + 4 * g, 0, g % 2, 4, x_hi, x_lo, (x_ready, 3 * KT))

            gate_product(0)
            for h in range(HEADS):
                statistic(head_stat[h], head_sq[h], sum_done, 9 + h)
            for g in range(1, HEADS):
                gate_product(g)
            residual_product(C_GLA_OUT, U_GLA_OUT, h_hi, h_lo, (hid_ready, HID_GLA), True)
            ffn(1, 4 * KT, 16)

            def output_rows(g, a):
                for b in range(4):
                    pe.wait_ge(xn_done, 2 * KT + 4 * g + b + 1)
                    ins = nc.tensor.transpose(out_bank[g][a][:, b * P:(b + 1) * P], act[:, 4 * g + b, a * P:(a + 1) * P],
                                              ident[:, :])
                return ins

            free_slot(0, U_OUT // 2)
            output_rows(0, 0)
            output_rows(0, 1).then_inc(out_t, 1)
            output_rows(1, 0)
            output_rows(1, 1).then_inc(out_t, 1)
            output_rows(2, 0).then_inc(out_t, 1)
            pe.wait_ge(sum_done, 20)
            for a in range(2):
                ins = mm(stat[:, 0, a:a + 1], sq_sum[:, a * P:(a + 1) * P], ones[:, 0:1], start=True, stop=True)
            ins.then_inc(stat_done, 1)
            free_slot(1, U_OUT // 2)
            output_rows(3, 0)
            output_rows(3, 1).then_inc(out_t, 1)
            pe.wait_ge(root_done, 10)
            output_rows(2, 1).then_inc(out_t, 1)


_INS = ["x", "norm_mix_g", "norm_ffn_g", "conv_w_in", "conv_b_in", "conv_w_dw", "conv_b_dw", "conv_ln_g", "conv_ln_b",
        "conv_w_out", "conv_b_out", "gla_w_in", "gla_gate_w1", "gla_gate_w2", "gla_gate_b", "gla_head_norm_g",
        "gla_w_out", "ffn_w_gate_up", "ffn_w_down", "final_norm_g"]


def kernel(**inputs):
    import numpy as _np
    import concourse.bacc as _bacc
    from concourse.bass_utils import run_bass_kernel_spmd as _run

    nc = _bacc.Bacc("TRN2", target_bir_lowering=False, num_devices=1)
    arrays, args = {}, []
    for name in _INS:
        a = _np.ascontiguousarray(inputs[name])
        arrays[f"in_{name}"] = a
        args.append(nc.dram_tensor(f"in_{name}", a.shape, mybir.dt.from_np(a.dtype), kind="ExternalInput").ap())
    args.append(nc.dram_tensor("out_0", (1, T, D), F32, kind="ExternalOutput").ap())
    trunk(nc, *args)
    r = _run(nc, [arrays], core_ids=[0])
    return r.results[0]["out_0"]
```
